# Optimizing a Trainium2 kernel written in Bass

```python
import jax, jax.numpy as jnp
from jax import lax
import numpy as np

D_MODEL = 1024
BATCH = 1
SEQ = 512
DEPTH = 1

ATT_HEADS = 8
ATT_HEAD_DIM = 64
IDX_HEADS = 8
IDX_HEAD_DIM = 64
TOPK_MAX = 256
Q_BLOCK = 128
RET_HEADS = 4
RET_HEAD_DIM = 128
RET_CHUNK = 128
ROPE_THETA = 10000.0
ATT_WIDTH = ATT_HEADS * ATT_HEAD_DIM
RET_WIDTH = RET_HEADS * RET_HEAD_DIM
MIX_WIDTH = ATT_WIDTH + RET_WIDTH
IN_SPLITS = (ATT_WIDTH, ATT_WIDTH, ATT_WIDTH, IDX_HEADS * IDX_HEAD_DIM, IDX_HEAD_DIM, IDX_HEADS,
             RET_WIDTH, RET_WIDTH, RET_WIDTH, RET_WIDTH)
IN_WIDTH = sum(IN_SPLITS)
N_GROUPS = 4
EXPERTS_PER_GROUP = 8
N_EXPERTS = N_GROUPS * EXPERTS_PER_GROUP
EXPERT_TOPK = 2
D_EXPERT = 256
N_MOD = 6
EPS = 1e-6

kernel_name = 'hybrid_dsa_retention_hmoe_block'

def _rms_norm(x, g=None):
    xf = x.astype(jnp.float32)
    y = xf * lax.rsqrt(jnp.mean(xf * xf, axis=-1, keepdims=True) + EPS)
    if g is not None:
        y = y * g.astype(jnp.float32)
    return y.astype(x.dtype)

def _rope(x, positions):
    d = x.shape[-1]
    half = d // 2
    freqs = ROPE_THETA ** (-jnp.arange(half, dtype=jnp.float32) / half)
    ang = positions.astype(jnp.float32)[..., None] * freqs
    cos = jnp.cos(ang)[:, :, None, :]
    sin = jnp.sin(ang)[:, :, None, :]
    xf = x.astype(jnp.float32)
    x1, x2 = xf[..., :half], xf[..., half:]
    return jnp.concatenate([x1 * cos - x2 * sin, x2 * cos + x1 * sin], axis=-1).astype(x.dtype)

def _dsa_sparse_attention(q, k, v, q_idx, k_idx, w_idx):
    B, S, H, dh = q.shape
    topk = min(TOPK_MAX, S // 4)
    nblk = S // Q_BLOCK
    key_pos = jnp.arange(S)
    bidx = jnp.arange(B)[:, None, None]
    k_idx_f = k_idx.astype(jnp.float32)

    def to_blocks(a):
        return a.reshape(B, nblk, Q_BLOCK, *a.shape[2:]).swapaxes(0, 1)

    def block_fn(args):
        qb, qib, wb, blk = args
        qpos = blk * Q_BLOCK + jnp.arange(Q_BLOCK)
        logits = jnp.einsum('bqhd,bsd->bqhs', qib.astype(jnp.float32), k_idx_f)
        score = jnp.einsum('bqh,bqhs->bqs', wb.astype(jnp.float32), jax.nn.relu(logits))
        causal = key_pos[None, :] <= qpos[:, None]
        score = jnp.where(causal[None], score, -jnp.inf)
        _, sel = lax.top_k(score, topk)
        valid = sel <= qpos[None, :, None]
        k_sel = k[bidx, sel].astype(jnp.float32)
        v_sel = v[bidx, sel].astype(jnp.float32)
        att = jnp.einsum('bqhd,bqkhd->bqhk', qb.astype(jnp.float32), k_sel) * (dh ** -0.5)
        att = jnp.where(valid[:, :, None, :], att, -jnp.inf)
        p = jax.nn.softmax(att, axis=-1)
        return jnp.einsum('bqhk,bqkhd->bqhd', p, v_sel).astype(q.dtype)

    out = lax.map(block_fn, (to_blocks(q), to_blocks(q_idx), to_blocks(w_idx), jnp.arange(nblk)))
    return out.swapaxes(0, 1).reshape(B, S, H, dh)

def _retention(q, k, v):
    B, S, H, d = q.shape
    C = RET_CHUNK
    N = S // C
    log_gamma = jnp.log(1.0 - 2.0 ** (-5.0 - jnp.arange(H, dtype=jnp.float32)))
    qf = q.astype(jnp.float32).reshape(B, N, C, H, d)
    kf = (k.astype(jnp.float32) * (d ** -0.5)).reshape(B, N, C, H, d)
    vf = v.astype(jnp.float32).reshape(B, N, C, H, d)
    idx = jnp.arange(C, dtype=jnp.float32)
    diff = idx[:, None] - idx[None, :]
    causal = diff >= 0
    decay = jnp.where(causal[None], jnp.exp(log_gamma[:, None, None] * jnp.where(causal, diff, 0.0)[None]), 0.0)
    inner = jnp.einsum('bnihd,bnjhd->bnhij', qf, kf) * decay[None, None]
    o_inner = jnp.einsum('bnhij,bnjhe->bnihe', inner, vf)
    k_decay = jnp.exp(log_gamma[None, :] * (C - 1 - idx)[:, None])
    kv = jnp.einsum('bnjhd,bnjhe->nbhde', kf * k_decay[:, :, None], vf)
    chunk_decay = jnp.exp(log_gamma * C)[None, :, None, None]

    def step(R, kv_n):
        return R * chunk_decay + kv_n, R

    _, R_prev = lax.scan(step, jnp.zeros((B, H, d, d), jnp.float32), kv)
    q_decay = jnp.exp(log_gamma[None, :] * (idx + 1.0)[:, None])
    o_cross = jnp.einsum('bnihd,nbhde->bnihe', qf * q_decay[:, :, None], R_prev)
    return (o_inner + o_cross).reshape(B, S, H, d)

def _hybrid_mixer(h, positions, w_in, w_out):
    B, S, _ = h.shape
    proj = jnp.einsum('bsd,de->bse', h, w_in)
    offsets = [int(o) for o in np.cumsum(IN_SPLITS)[:-1]]
    q_a, k_a, v_a, q_i, k_i, w_i, q_r, k_r, v_r, g_r = jnp.split(proj, offsets, axis=-1)
    q_a = _rope(q_a.reshape(B, S, ATT_HEADS, ATT_HEAD_DIM), positions)
    k_a = _rope(k_a.reshape(B, S, ATT_HEADS, ATT_HEAD_DIM), positions)
    v_a = v_a.reshape(B, S, ATT_HEADS, ATT_HEAD_DIM)
    q_i = _rope(q_i.reshape(B, S, IDX_HEADS, IDX_HEAD_DIM), positions)
    k_i = _rope(k_i[:, :, None, :], positions)[:, :, 0, :]
    w_i = w_i * ((IDX_HEADS ** -0.5) * (IDX_HEAD_DIM ** -0.5))
    att = _dsa_sparse_attention(q_a, k_a, v_a, q_i, k_i, w_i).reshape(B, S, ATT_WIDTH)
    q_r = _rope(q_r.reshape(B, S, RET_HEADS, RET_HEAD_DIM), positions)
    k_r = _rope(k_r.reshape(B, S, RET_HEADS, RET_HEAD_DIM), positions)
    v_r = v_r.reshape(B, S, RET_HEADS, RET_HEAD_DIM)
    ret = _rms_norm(_retention(q_r, k_r, v_r)).reshape(B, S, RET_WIDTH)
    ret = (jax.nn.silu(g_r.astype(jnp.float32)) * ret).astype(h.dtype)
    mixed = jnp.concatenate([att.astype(h.dtype), ret], axis=-1)
    return jnp.einsum('bse,ed->bsd', mixed, w_out)

def _hier_moe(h, w_group, b_group, w_expert, b_expert, w_gate_exp, w_up_exp, w_down_exp):
    B, S, D = h.shape
    T = B * S
    t = h.reshape(T, D)
    g_prob = jax.nn.softmax((t @ w_group + b_group).astype(jnp.float32), axis=-1)
    g_top, g_sel = lax.top_k(g_prob, 1)
    e_logits = (t @ w_expert + b_expert).astype(jnp.float32).reshape(T, N_GROUPS, EXPERTS_PER_GROUP)
    e_logits = jnp.take_along_axis(e_logits, g_sel[:, :, None], axis=1)[:, 0]
    e_top, e_sel = lax.top_k(jax.nn.softmax(e_logits, axis=-1), EXPERT_TOPK)
    weights = g_top * e_top / jnp.sum(e_top, axis=-1, keepdims=True)
    expert_id = g_sel * EXPERTS_PER_GROUP + e_sel
    combine = jnp.einsum('tk,tke->te', weights, jax.nn.one_hot(expert_id, N_EXPERTS, dtype=jnp.float32))
    y = jnp.zeros((T, D), jnp.float32)
    for e in range(N_EXPERTS):
        hid = jax.nn.silu(t @ w_gate_exp[e]) * (t @ w_up_exp[e])
        y = y + combine[:, e:e + 1] * (hid @ w_down_exp[e]).astype(jnp.float32)
    return y.astype(h.dtype).reshape(B, S, D)

def setup_inputs(seed: int = 0) -> dict:
    key = jax.random.key(seed)
    ks = jax.random.split(key, 20)
    f32 = jnp.float32
    nrm = lambda k, shape, s: jax.random.normal(k, shape, f32) * s
    L = DEPTH
    x = jax.random.normal(ks[0], (BATCH, SEQ, D_MODEL), f32)
    c = jax.random.normal(ks[1], (BATCH, D_MODEL), f32)
    positions = (jax.random.randint(ks[2], (BATCH, 1), 0, 1024) + jnp.arange(SEQ)[None, :]).astype(jnp.int32)
    return {
        'x': x,
        'c': c,
        'positions': positions,
        'g_pre_mix': 1.0 + nrm(ks[3], (L, D_MODEL), 0.05),
        'w_ada': nrm(ks[4], (L, D_MODEL, N_MOD * D_MODEL), 0.5 * D_MODEL ** -0.5),
        'b_ada': nrm(ks[5], (L, N_MOD * D_MODEL), 0.02),
        'w_in': nrm(ks[6], (L, D_MODEL, IN_WIDTH), D_MODEL ** -0.5),
        'w_out': nrm(ks[7], (L, MIX_WIDTH, D_MODEL), MIX_WIDTH ** -0.5),
        'g_post_mix': 1.0 + nrm(ks[8], (L, D_MODEL), 0.05),
        'g_pre_ffn': 1.0 + nrm(ks[9], (L, D_MODEL), 0.05),
        'w_group': nrm(ks[10], (L, D_MODEL, N_GROUPS), D_MODEL ** -0.5),
        'b_group': nrm(ks[11], (L, N_GROUPS), 0.01),
        'w_expert': nrm(ks[12], (L, D_MODEL, N_EXPERTS), D_MODEL ** -0.5),
        'b_expert': nrm(ks[13], (L, N_EXPERTS), 0.01),
        'w_gate_exp': nrm(ks[14], (L, N_EXPERTS, D_MODEL, D_EXPERT), D_MODEL ** -0.5),
        'w_up_exp': nrm(ks[15], (L, N_EXPERTS, D_MODEL, D_EXPERT), D_MODEL ** -0.5),
        'w_down_exp': nrm(ks[16], (L, N_EXPERTS, D_EXPERT, D_MODEL), D_EXPERT ** -0.5),
        'g_post_ffn': 1.0 + nrm(ks[17], (L, D_MODEL), 0.05),
    }

def reference(x, c, positions, g_pre_mix, w_ada, b_ada, w_in, w_out, g_post_mix, g_pre_ffn,
              w_group, b_group, w_expert, b_expert, w_gate_exp, w_up_exp, w_down_exp, g_post_ffn):
    h_res = x
    for l in range(DEPTH):
        mod = jax.nn.silu(c) @ w_ada[l] + b_ada[l]
        shift1, scale1, gate1, shift2, scale2, gate2 = [m[:, None, :] for m in jnp.split(mod, N_MOD, axis=-1)]
        h = _rms_norm(h_res, g_pre_mix[l]) * (1.0 + scale1) + shift1
        mix = _hybrid_mixer(h, positions, w_in[l], w_out[l])
        h_res = (h_res + gate1 * _rms_norm(mix, g_post_mix[l])).astype(x.dtype)
        h2 = _rms_norm(h_res, g_pre_ffn[l]) * (1.0 + scale2) + shift2
        ffn = _hier_moe(h2, w_group[l], b_group[l], w_expert[l], b_expert[l],
                        w_gate_exp[l], w_up_exp[l], w_down_exp[l])
        h_res = (h_res + gate2 * _rms_norm(ffn, g_post_ffn[l])).astype(x.dtype)
    return h_res


_drawn_inputs = setup_inputs


def setup_inputs(seed=0):
    import zlib

    import numpy as np

    out = dict(_drawn_inputs(seed))
    spreads = {}
    factors = {'b_group': 3.057, 'b_expert': 2.802, 'g_post_ffn': 3.832}
    for name, (base, spread) in spreads.items():
        noise = np.random.default_rng([zlib.crc32(name.encode()), seed]).standard_normal(out[name].shape)
        drawn = base * np.exp(spread * noise) if base else spread * noise
        out[name] = __import__('jax').numpy.asarray(drawn.astype(out[name].dtype))
    for name, factor in factors.items():
        out[name] = (out[name] * factor).astype(out[name].dtype)
    return out
```

```python
from contextlib import ExitStack
import math

import numpy as np
import concourse.bass as bass
from concourse import mybir

P = 128
D = 1024
S = 512
NB = S // P
KD = D // P
HEADS, DH = 8, 64
RHEADS, RDH = 4, 128
TOPK = min(256, S // 4)
NG, EPG = 4, 8
NE = NG * EPG
F = 256
KF = F // P
EPS = 1e-6
NEG = -1.0e30
TAKEN = -3.0e38
IDX_SCALE = (HEADS ** -0.5) * (DH ** -0.5)
ATT_SCALE = DH ** -0.5
MAGIC = 1.5 * 2.0 ** 23

TWO_PI = (6.28125, 0.0019350051879882812, 3.019916050268e-07)
CAP = 96
NOV = 2 * S // CAP
NT = NE + NOV
NM = (S + CAP - 1) // CAP
NOBODY = 8 * S
RING = 4
CHUNK = KD * 512
SLOT = KD * F * 2 + KF * D

ALU = mybir.AluOpType
ACT = mybir.ActivationFunctionType
AX = mybir.AxisListType.X
F32 = mybir.dt.float32
I32 = mybir.dt.int32
U32 = mybir.dt.uint32

COL = {"qa": 0, "ka": 512, "va": 1024, "qi": 1536, "kw": 2048, "qr": 2120, "kr": 2632, "vr": 3144, "gr": 3656}
KW = DH + HEADS
ROPE = {"kw": DH, "qi": DH, "qa": DH, "ka": DH, "qr": RDH, "kr": RDH}
ITEMS = ([("ada", 0), ("ada", 1), ("ada", 2), ("ada", 3), ("in", "kw"), ("in", "qi"), ("ada", 4), ("in", "qr"),
          ("ada", 5), ("in", "kr"), ("ada", 6), ("in", "vr"), ("ada", 7), ("in", "gr"), ("ada", 8), ("in", "ka"),
          ("ada", 9), ("in", "qa"), ("ada", 10), ("in", "va"), ("ada", 11), ("out", 0), ("out", 1), ("router", 0)])
AT = {item: n for n, item in enumerate(ITEMS)}
assert len(ITEMS) % RING == 0 and NE % RING == 0
EARLY = len(ITEMS) // RING

C_ID, C_CAUSAL, C_LT, C_ONES, C_FREQ, C_EIDX, C_OIDX = 0, 128, 256, 384, 512, 576, 608
C_EPS = 624
NCONST = 625


def shape_constants():
    c = np.zeros((P, NCONST), np.float32)
    i = np.arange(P)
    c[:, C_ID:C_ID + P] = np.eye(P)
    c[:, C_CAUSAL:C_CAUSAL + P] = np.where(i[None, :] <= i[:, None], 0.0, NEG)
    c[:, C_LT:C_LT + P] = i[:, None] < i[None, :]
    c[:, C_ONES:C_ONES + P] = 1.0
    c[:, C_FREQ:C_FREQ + 64] = np.float32(10000.0) ** (-np.arange(64, dtype=np.float32) / np.float32(64))
    c[:, C_EIDX:C_EIDX + NE] = np.arange(NE)
    c[:, C_OIDX:C_OIDX + 16] = np.arange(16)
    c[:, C_EPS] = EPS
    g = 1.0 - 2.0 ** (-5.0 - np.arange(RHEADS))
    diff = np.arange(S)[None, None, :] - i[:, None, None]
    decay = np.where(diff >= 0, np.exp(np.log(g)[None, :, None] * np.maximum(diff, 0)), 0.0) * RDH ** -0.5
    pair = ((np.arange(NB)[None, :, None] * P + i[:, None, None]) * 2 + np.arange(2)[None, None, :])
    return c, decay.reshape(P, RHEADS * S).astype(np.float32), pair.reshape(P, 2 * NB).astype(np.int32)


ORDER = ["kw", "qi", "qr", "IDX", "kr", ("MOD", 2), "vr", "gr", ("MOD", 3), "ka", "RET", "qa", ("MOD", 4), "va",
         "RETT", "ATT", ("MOD", 5), "OUT"]
AHEADS = [(b, h) for b in range(NB) for h in range(HEADS)]


class Plan:

    def __init__(self):
        self.bank, self.before, last = {}, {}, {}
        self.tp, self.sc, self.rope, self.unit, self.o = {}, {}, {}, {}, 0
        self.v = {}

        def use(name, bank, width=1):
            self.bank[name] = bank
            self.before[name] = [last[b] for b in range(bank, bank + width) if b in last]
            for b in range(bank, bank + width):
                last[b] = name

        def turn(name):
            self.tp[name] = len(self.tp)
            use(name, 2 + self.tp[name] % 2)

        def score(name):
            self.sc[name] = len(self.sc)
            use(name, 4 + self.sc[name] % 2)

        def output(name):
            use(name, 6 + self.o % 2)
            self.o += 1

        self.steps = []
        waiting = None
        output(("modA",))
        for k in range(KD):
            turn(("x", k))
        for s in ORDER:
            if s in COL:
                for b in range(NB):
                    name = ("unit", s, b)
                    self.unit[name] = len(self.unit)
                    use(name, self.unit[name] % 2)
                    self.steps.append(name)
                    if waiting:
                        turn(waiting)
                        self.steps.append(waiting)
                        waiting = None
                    if s in ROPE:
                        self.rope[name] = len(self.rope)
                        waiting = ("turn", s, b)
                    if s in ("vr", "va"):
                        self.v[name] = len(self.v)
                continue
            s = s if isinstance(s, tuple) else (s,)
            self.steps.append(s)
            if s[0] == "MOD":
                output(s + (0,))
                output(s + (1,))
            elif s[0] == "IDX":
                for b in range(1, NB):
                    for h in range(HEADS):
                        score(("idx", b, h))
            elif s[0] == "RET":
                for h in range(RHEADS):
                    for j in range(NB):
                        score(("ret", h, j))
                    output(("reto", h))
            elif s[0] == "RETT":
                for b in range(NB):
                    turn(("rett", b))
            elif s[0] == "ATT":
                for u in range(len(AHEADS) + 4):
                    if u < len(AHEADS):
                        score(("att",) + AHEADS[u])
                    if 2 <= u < len(AHEADS) + 2:
                        turn(("pt",) + AHEADS[u - 2])
                    if 3 <= u < len(AHEADS) + 3 and AHEADS[u - 3][1] == 0:
                        output(("atto", AHEADS[u - 3][0]))
                    if u >= 4 and AHEADS[u - 4][1] == HEADS - 1:
                        turn(("attt", AHEADS[u - 4][0]))
            elif s[0] == "OUT":
                for b in range(NB):
                    use(("wout", b), (0, 6)[b % 2], 2)
                for b in range(NB):
                    turn(("h2", b, 0))
                    turn(("h2", b, 1))
                use(("router",), 4)
                use(("rank",), 5)


def build(nc, t, out):
    plan = Plan()
    steps = plan.steps

    with ExitStack() as ctx:
        def sb(name, words, dt=F32, parts=P):
            return ctx.enter_context(nc.sbuf_tensor(name, [parts, words], dt))

        def sem(name):
            return ctx.enter_context(nc.semaphore(name))

        psum = ctx.enter_context(nc.psum_tensor("psum", [P, 8 * 512], F32))
        ps = [psum[:, i * 512:(i + 1) * 512] for i in range(8)]

        ring = sb("ring", RING * SLOT)
        xs = sb("xs", NB * D)
        hT = sb("hT", KD * S)
        work = sb("work", 4 * 2048 + 512)
        retbuf = sb("retbuf", 2560)
        ropebuf = sb("ropebuf", 2048)
        accB = sb("accB", D)
        G1 = sb("G1", D)
        S2 = sb("S2", D)
        T2 = sb("T2", D)
        score = sb("score", P * (2 + 3 + 4))
        cst = sb("cst", NCONST)
        cosT = sb("cosT", NB * 64)
        sinT = sb("sinT", NB * 64)
        sm = sb("sm", 256)
        rb = sb("rb", 36)
        posi = sb("posi", NB, I32)
        pairc = sb("pairc", 2 * NB, I32)
        addr_i = sb("addr_i", 2 * NB, U32)
        pid_t = sb("pid_t", NT, U32)
        tok_t = sb("tok_t", NT, U32)
        ctl = sb("ctl", NOV + 1, I32)
        gix = sb("gix", 2, U32)
        six = sb("six", 2, U32)

        x3 = xs[:, :].rearrange("p (b d) -> p b d", b=NB)
        hT3 = hT[:, :].rearrange("p (k t) -> p k t", k=KD)
        ident = cst[:, C_ID:C_ID + P]
        ones = cst[:, C_ONES:C_ONES + P]

        qaT = work[:, 0:2048].rearrange("p (c t) -> p c t", c=4)
        kaT = work[:, 2048:4096].rearrange("p (c t) -> p c t", c=4)
        va = work[:, 4096:6144].rearrange("p (b e) -> p b e", b=NB)
        qiT = work[:, 6144:8192].rearrange("p (c t) -> p c t", c=4)
        kiT = work[:, 8192:8704]
        decay = work[:, 0:2048].rearrange("p (h t) -> p h t", h=RHEADS)
        xn = work[:, 0:4096].rearrange("p (b d) -> p b d", b=NB)
        accA = work[:, 4096:6144].rearrange("p (m n) -> p m n", m=2)
        Rsb = work[:, 6144:8192].rearrange("p (b e) -> p b e", b=NB)

        def tail(s):
            return ring[:, s * SLOT + CHUNK:(s + 1) * SLOT]
        qrT = tail(0).rearrange("p (c t) -> p c t", c=4)
        krT = tail(1).rearrange("p (c t) -> p c t", c=4)
        vr = tail(2).rearrange("p (b e) -> p b e", b=NB)
        gr = tail(3).rearrange("p (b e) -> p b e", b=NB)

        def chunk(n, cols=512):
            s = n % RING
            return ring[:, s * SLOT:s * SLOT + KD * cols].rearrange("p (k n) -> p k n", k=KD)

        def expert(s):
            base = s * SLOT
            w = KD * F
            return (ring[:, base:base + w].rearrange("p (k n) -> p k n", k=KD),
                    ring[:, base + w:base + 2 * w].rearrange("p (k n) -> p k n", k=KD),
                    ring[:, base + 2 * w:base + SLOT].rearrange("p (i n) -> p i n", i=KF))

        def cols(at, n):
            return sm[:, at:at + n]
        cc, sc_, cg, cb = cols(0, 8), cols(8, 8), cols(16, 8), cols(24, 16)
        gs1, sh1 = cols(40, 8), cols(48, 8)
        ss1, r1 = cols(56, 4), cols(60, 4)
        posf = cols(64, 4)
        wi = cols(68, 32).rearrange("p (b h) -> p b h", b=NB)
        ssr, rr = cols(100, 16), cols(116, 16)
        nmx, rsum, rinv = cols(132, 2), cols(134, 32).rearrange("p (b h) -> p b h", b=NB), cols(166, 8)
        ssm, rm = cols(174, 4), cols(186, 4)
        ss2, r2 = cols(190, 4), cols(194, 4)
        wts = cols(198, 8).rearrange("p (b j) -> p b j", b=NB)
        ctmp = cols(206, 16)
        modA_s = cols(222, 16)
        yss, yr = cols(238, 4), cols(242, 4)
        top8 = cols(248, 8)

        x_in, params_in, decay_in = sem("x_in"), sem("params_in"), sem("decay_in")
        landed = [sem(f"landed{s}") for s in range(RING)]
        ada_done = sem("ada_done")
        v_chain, a_chain, p_chain = sem("v_chain"), sem("a_chain"), sem("p_chain")
        c_exp, c_silu = sem("c_exp"), sem("c_silu")
        x_ss, x_sq, x_n = sem("x_ss"), sem("x_sq"), sem("x_n")
        wout_done = sem("wout_done")
        ang_ready, trig_ready = sem("ang_ready"), sem("trig_ready")
        modA_done, gs_ready = sem("modA_done"), sem("gs_ready")
        unit_done, tp_done, sc_done, o_done = sem("unit_done"), sem("tp_done"), sem("sc_done"), sem("o_done")
        rope_ab, roped = sem("rope_ab"), sem("roped")
        evac = sem("evac")
        v_ready = sem("v_ready")
        g_exp, g_ready = sem("g_exp"), sem("g_ready")
        relu_ready, relu_used = sem("relu_ready"), sem("relu_used")
        mod_done, mod_ready = sem("mod_done"), sem("mod_ready")
        it_ready, it_used = sem("it_ready"), sem("it_used")
        R_ready, ret_ss, ret_sq, ret_ready = sem("R_ready"), sem("ret_ss"), sem("ret_sq"), sem("ret_ready")
        att_max, att_exp = sem("att_max"), sem("att_exp")
        att_ready = sem("att_ready")
        mix_ss, mix_sq, mix_n = sem("mix_ss"), sem("mix_sq"), sem("mix_n")
        res_ready, res_ss, res_sq = sem("res_ready"), sem("res_ss"), sem("res_sq")
        h2_a, h2_ready = sem("h2_a"), sem("h2_ready")
        h2_out = [sem("h2_out0"), sem("h2_out1")]
        g_sub, g_exped, d_sub, d_exped = sem("g_sub"), sem("g_exped"), sem("d_sub"), sem("d_exped")
        oh_ready, rank_done, addr_ready, tab_init, tab_set, tab_in, tok_ready = (
            sem("oh_ready"), sem("rank_done"), sem("addr_ready"), sem("tab_init"), sem("tab_set"), sem("tab_in"),
            sem("tok_ready"))
        router_done = sem("router_done")
        tab_fill = sem("tab_fill")
        xg_in = [sem("xg_in0"), sem("xg_in1")]
        xg_clear, xt_mm, xt_ev = sem("xg_clear"), sem("xt_mm"), sem("xt_ev")
        gu_mm, gu_exp, gu_step, hid_ready = sem("gu_mm"), sem("gu_exp"), sem("gu_step"), sem("hid_ready")
        y_mm, y_evA, y_evV = sem("y_mm"), sem("y_evA"), sem("y_evV")
        y_out = [sem("y_out0"), sem("y_out1")]
        yw_ready, y_ss, y_sq, o_mul, o_add = (
            sem("yw_ready"), sem("y_ss"), sem("y_sq"), sem("o_mul"), sem("o_add"))
        y_back = [sem("y_back0"), sem("y_back1")]
        o_out = [sem("o_out0"), sem("o_out1")]
        lg_ready, ix_ready = sem("lg_ready"), sem("ix_ready")
        nobody_set = sem("nobody_set")
        pool_steps = sem("pool_steps")
        ctl_ready, ov_go, ov_w, ov_x, ov_turned, ov_brought = (sem("ctl_ready"), sem("ov_go"), sem("ov_w"),
                                                               sem("ov_x"), sem("ov_turned"), sem("ov_brought"))
        ov_gu, ov_exp, ov_step, ov_hid, ov_y, ov_evA, ov_evV, ov_ix, ov_out = (
            sem("ov_gu"), sem("ov_exp"), sem("ov_step"), sem("ov_hid"), sem("ov_y"), sem("ov_evA"), sem("ov_evV"),
            sem("ov_ix"), sem("ov_out"))
        g2_in, accB_clear, bias_in = sem("g2_in"), sem("accB_clear"), sem("bias_in")
        y_base = sem("y_base")

        h2_dram = nc.dram_tensor("h2_rows", [S, D], F32, kind="Internal").ap()
        y_dram = nc.dram_tensor("pair_rows", [2 * S, D], F32, kind="Internal").ap()
        tab_dram = nc.dram_tensor("slot_table", [CAP * NT, 1], U32, kind="Internal").ap()
        tab_rows = tab_dram.rearrange("(c t) a -> c (t a)", c=CAP)

        w_ada = t["w_ada"].rearrange("l (p k) n -> (l p) k n", k=KD)
        w_in = t["w_in"].rearrange("l (p k) n -> (l p) k n", k=KD)
        w_out = t["w_out"].rearrange("l (k p) n -> (l p) k n", k=KD)
        w_grp = t["w_group"].rearrange("l (p k) n -> (l p) k n", k=KD)
        w_exp = t["w_expert"].rearrange("l (p k) n -> (l p) k n", k=KD)
        wg_d = t["w_gate_exp"].rearrange("l e (p k) n -> (l e) p (k n)", k=KD)
        wu_d = t["w_up_exp"].rearrange("l e (p k) n -> (l e) p (k n)", k=KD)
        wd_d = t["w_down_exp"].rearrange("l e (p i) n -> (l e) p (i n)", i=KF)
        b_ada = t["b_ada"].rearrange("l (m n) -> (l m) n", n=D)

        def pcol(name):
            return t[name].rearrange("l (p k) -> (l p) k", k=KD)

        def prow(ap, n):
            return ap.broadcast_to([P, n])

        block = ctx.enter_context(nc.Block())

        def bank(use):
            return ps[plan.bank[use]]

        def read_out(use):
            kind = use[0]
            if use in plan.tp:
                return evac, plan.tp[use] + 1
            if use in plan.rope:
                return rope_ab, plan.rope[use] + 1
            if use in plan.v:
                return v_ready, plan.v[use] + 1
            if kind == "unit":
                return g_ready, use[2] + 1
            return {"modA": lambda: (gs_ready, 2),
                    "MOD": lambda: (mod_ready, 2 * (use[1] - 2) + use[2] + 1),
                    "idx": lambda: (relu_ready, plan.sc[use] + 1),
                    "ret": lambda: (it_ready, NB * use[1] + use[2] + 1),
                    "reto": lambda: (R_ready, use[1] + 1),
                    "att": lambda: (att_max, use[1] * HEADS + use[2] + 1),
                    "atto": lambda: (att_ready, use[1] + 1),
                    "wout": lambda: (mix_n, use[1] + 1)}[kind]()

        def take(pe, use):
            for earlier in plan.before[use]:
                pe.wait_ge(*read_out(earlier))
            return ps[plan.bank[use]]

        def used_up(item):
            kind, what = item
            if kind == "ada":
                return ada_done, what + 1
            if kind == "in":
                return unit_done, plan.unit[("unit", what, NB - 1)] + 1
            return (wout_done, NB) if kind == "out" else (router_done, NB)

        def brought(use):
            return evac, plan.tp[use] + 1

        XG = [hT[0:CAP, i * D:(i + 1) * D] for i in range(2)]
        XT = [hT[:, 2 * D + i * KD * CAP:2 * D + (i + 1) * KD * CAP].rearrange("p (k c) -> p k c", k=KD)
              for i in range(2)]
        YO = [work[0:CAP, i * D:(i + 1) * D] for i in range(2)]
        W2 = KF * CAP
        EG = [work[:, 2048 + i * W2:2048 + (i + 1) * W2] for i in range(2)]
        HID = [work[:, 2048 + (2 + i) * W2:2048 + (3 + i) * W2].rearrange("p (i c) -> p i c", i=KF) for i in range(2)]
        GUM = work[:, 2048 + 4 * W2:2048 + 5 * W2]
        YG = [work[:, 4096 + i * 2 * D:4096 + (i + 1) * 2 * D].rearrange("p (j d) -> p j d", j=2) for i in range(2)]

        def load_expert(sp, e, s, signal=None):
            signal = signal or landed[s]
            w = KD * F
            base = s * SLOT
            sp.dma_start(ring[:, base:base + w], pick(wg_d, e)).then_inc(signal, 16)
            sp.dma_start(ring[:, base + w:base + 2 * w], pick(wu_d, e)).then_inc(signal, 16)
            sp.dma_start(ring[:, base + 2 * w:base + SLOT], pick(wd_d, e)).then_inc(signal, 16)

        def pick(ap, e):
            return ap[e, :, :] if isinstance(e, int) else ap[bass.ds(e, 1), :, :].rearrange("a p n -> (a p) n")

        def land(eng, n):
            extra = 16 if n == AT[("router", 0)] else 0
            eng.wait_ge(landed[n % RING], 16 * (n // RING + 1) + extra)

        def landed_by(e, s):
            early = 16 * EARLY + (16 if s == AT[("router", 0)] % RING else 0)
            return early + 12 * (e - s) + 48

        def iT(h, j):
            at = (0, 512, 896, 1152)[j] + (h % 2) * 1280
            return retbuf[:, at:at + S - j * P]

        PARAMS = 16 * 10
        eps = cst[:, C_EPS:C_EPS + 1]

        def each_overflow(eng, work_on):
            eng.wait_ge(ctl_ready, 1)
            count = eng.value_load(ctl[0:1, NOV:NOV + 1], min_val=0, max_val=NOV)
            with eng.If(count > 0):
                with eng.Fori(0, count) as o:
                    work_on(o)

        RELU = [retbuf[:, i * 512:(i + 1) * 512] for i in range(2)]
        SMX = [ropebuf[:, i * 512:(i + 1) * 512] for i in range(2)]
        PEX = [ropebuf[:, 1024 + i * 512:1536 + i * 512] for i in range(2)]
        ATO = [retbuf[:, i * 512:(i + 1) * 512] for i in range(2)]
        PTS = [retbuf[:, 1024 + i * 512:1536 + i * 512] for i in range(2)]
        MIXN = [work[:, i * D:(i + 1) * D] for i in range(2)]
        H2 = [work[:, i * D:(i + 1) * D] for i in (2, 7)]
        G2 = work[:, 3 * D:4 * D]
        H2T = [work[:, (4 + i) * D:(5 + i) * D].rearrange("p (k t) -> p k t", k=KD) for i in range(2)]
        JUNK = work[:, 6 * D:7 * D]
        JUNK2 = work[:, 0:D]
        out_blocks = out.rearrange("a (b p) d -> (a b) p d", p=P)
        def rt(at, n):
            return retbuf[:, at:at + NB * n].rearrange("p (b n) -> p b n", b=NB)
        LG, GMAX, GSUBV, GEXV, GSUM, GTOP = rt(0, 36), rt(144, 1), rt(152, NG), rt(168, NG), rt(184, 1), rt(188, 1)
        GT, GM, SG = rt(192, NG), rt(208, 1), rt(212, NG)
        OH = rt(256, NE)
        EL, EMAX, ET, EM, O1, EL2, EMAX2, O2 = (rt(512, EPG), rt(544, 1), rt(548, EPG), rt(580, 1), rt(584, EPG),
                                                rt(616, EPG), rt(648, 1), rt(652, EPG))
        DSUB, P2, WT = rt(684, 1), rt(688, 1), rt(692, 1)
        OH1, OH2, RANK = rt(704, NE), rt(832, NE), rt(960, NE)
        CNT, OV, BINC, BEX = (retbuf[:, 1088:1120], retbuf[:, 1248:1280], retbuf[:, 1280:1312], retbuf[:, 1312:1344])
        MFL, QT, ADR, TMP = rt(1120, NE), rt(1344, NE), rt(1472, NE), rt(1600, NE)
        POS = retbuf[:, 1728:1736].rearrange("p (b j) -> p b j", b=NB)
        OVC = retbuf[:, 1760:1760 + NOV * NE].rearrange("p (o e) -> p o e", o=NOV)
        EO = retbuf[:, 2400:2400 + NOV]

        @block.sync
        def _(sp):
            sp.dma_start(x3, t["x"].rearrange("a (b p) d -> (a p) b d", p=P)).then_inc(x_in, 16)
            for n, (kind, what) in enumerate(ITEMS):
                s = n % RING
                if n >= RING:
                    sp.wait_ge(*used_up(ITEMS[n - RING]))
                if kind == "ada":
                    sp.dma_start(chunk(n), w_ada[:, :, what * 512:(what + 1) * 512]).then_inc(landed[s], 16)
                elif kind == "in":
                    width = KW if what == "kw" else 512
                    sp.dma_start(chunk(n, width), w_in[:, :, COL[what]:COL[what] + width]).then_inc(landed[s], 16)
                elif kind == "out":
                    sp.dma_start(chunk(n), w_out[:, :, what * 512:(what + 1) * 512]).then_inc(landed[s], 16)
                else:
                    r = chunk(n, NG + NE)
                    sp.dma_start(r[:, :, 0:NG], w_grp).then_inc(landed[s], 16)
                    sp.dma_start(r[:, :, NG:NG + NE], w_exp).then_inc(landed[s], 16)
                if (kind, what) == ("in", "kw"):
                    sp.wait_ge(tp_done, KD)
                    sp.dma_start(work[:, 0:RHEADS * S], t["decay"]).then_inc(decay_in, 16)
            sp.wait_ge(ret_ready, NB)
            for e in range(RING):
                sp.wait_ge(*used_up(ITEMS[len(ITEMS) - RING + e]))
                load_expert(sp, e, e)
            with sp.Fori(1, NE // RING) as i:
                for j in range(RING):
                    sp.wait_ge(y_mm, i * 2 * RING + (2 * j + 2 - 2 * RING))
                    load_expert(sp, i * RING + j, j)
            sp.wait_ge(y_mm, 2 * NE)

            def overflow(o):
                sp.wait_ge(ov_go, o + 1)
                load_expert(sp, sp.value_load(ctl[0:1, bass.ds(o, 1)], min_val=0, max_val=NE - 1), 0, ov_w)
            each_overflow(sp, overflow)
            for b in range(NB):
                sp.wait_ge(o_add, b + 1)
                sp.dma_start(out_blocks[b], YG[b % 2][:, 1, :]).then_inc(o_out[b % 2], 16)
            for par in range(2):
                sp.wait_ge(o_out[par], 16 * NB // 2)

        @block.tensor
        def _(pe):
            def chunk_unit(name, b):
                n = AT[("in", name)]
                width = KW if name == "kw" else 512
                w = chunk(n, width)
                if b == 0:
                    land(pe, n)
                    if name == "kw":
                        pe.wait_ge(*brought(("x", KD - 1)))
                o = take(pe, ("unit", name, b))
                for k in range(KD):
                    mm = pe.matmul(o[:, 0:width], hT3[:, k, b * P:(b + 1) * P], w[:, k, :], start=(k == 0),
                                   stop=(k == KD - 1))
                mm.then_inc(unit_done, 1)

            def turn(name, b):
                use = ("turn", name, b)
                r = plan.rope[("unit", name, b)]
                o = take(pe, use)
                pe.wait_ge(roped, r + 1)
                src = ropebuf[:, 1024 + (r % 2) * 512:1536 + (r % 2) * 512]
                for c in range(1 if name == "kw" else 4):
                    mm = pe.transpose(o[:, c * P:(c + 1) * P], src[:, c * P:(c + 1) * P], ident)
                mm.then_inc(tp_done, 1)

            pe.wait_ge(params_in, PARAMS)
            pe.wait_ge(ada_done, 4)
            o = take(pe, ("modA",))
            for m in range(2):
                a = accA[:, m, :].rearrange("p (q k) -> p k q", k=KD)
                for k in range(KD):
                    mm = pe.matmul(o[:, m * KD + k:m * KD + k + 1], a[:, k, :], ones[:, 0:1], start=True, stop=True)
            mm.then_inc(modA_done, 1)
            pe.wait_ge(x_n, NB)
            for k in range(KD):
                o = take(pe, ("x", k))
                for b in range(NB):
                    v = xn[:, b, :].rearrange("p (q k) -> p k q", k=KD)
                    mm = pe.transpose(o[:, b * P:(b + 1) * P], v[:, k, :], ident)
                mm.then_inc(tp_done, 1)

            def mod(m):
                pe.wait_ge(ada_done, 2 * m + 2)
                for n in range(2):
                    o = take(pe, ("MOD", m, n))
                    pe.matmul(o[:, :], ones, accB[:, n * 512:(n + 1) * 512], start=True, stop=True).then_inc(mod_done, 1)

            def idx():
                pe.wait_ge(*brought(("turn", "qi", NB - 1)))
                for b in range(1, NB):
                    for h in range(HEADS):
                        n = (b + 1) * P
                        lo = DH * (h % 2)
                        o = take(pe, ("idx", b, h))
                        pe.matmul(o[:, 0:n], qiT[lo:lo + DH, h // 2, b * P:(b + 1) * P], kiT[lo:lo + DH, 0:n],
                                  start=True, stop=True).then_inc(sc_done, 1)

            def retention():
                pe.wait_ge(*brought(("turn", "kr", NB - 1)))
                pe.wait_ge(v_ready, NB)
                for h in range(RHEADS + 1):
                    if h < RHEADS:
                        for j in range(NB):
                            n = S - j * P
                            o = take(pe, ("ret", h, j))
                            pe.matmul(o[:, 0:n], krT[:, h, j * P:(j + 1) * P], qrT[:, h, j * P:S], start=True,
                                      stop=True).then_inc(sc_done, 1)
                    if h >= 1:
                        g = h - 1
                        o = take(pe, ("reto", g))
                        pe.wait_ge(it_ready, NB * (g + 1))
                        for i in range(NB):
                            for j in range(i + 1):
                                mm = pe.matmul(o[:, i * P:(i + 1) * P], iT(g, j)[:, (i - j) * P:(i - j + 1) * P],
                                               vr[:, j, g * RDH:(g + 1) * RDH], start=(j == 0), stop=(j == i))
                        mm.then_inc(o_done, 1)

            def retention_turn():
                for b in range(NB):
                    o = take(pe, ("rett", b))
                    pe.wait_ge(ret_ready, b + 1)
                    for c in range(4):
                        mm = pe.transpose(o[:, c * P:(c + 1) * P], Rsb[:, b, c * P:(c + 1) * P], ident)
                    mm.then_inc(tp_done, 1)

            def attention():
                def scores(b, h):
                    n = (b + 1) * P
                    lo = DH * (h % 2)
                    o = take(pe, ("att", b, h))
                    pe.matmul(o[:, 0:n], qaT[lo:lo + DH, h // 2, b * P:(b + 1) * P], kaT[lo:lo + DH, h // 2, 0:n],
                              start=True, stop=True).then_inc(sc_done, 1)

                def turn_p(b, h):
                    u = b * HEADS + h
                    o = take(pe, ("pt", b, h))
                    pe.wait_ge(att_exp, u + 1)
                    for j in range(b + 1):
                        mm = pe.transpose(o[:, j * P:(j + 1) * P], PEX[u % 2][:, j * P:(j + 1) * P], ident)
                    mm.then_inc(tp_done, 1)

                def values(b, h):
                    u = b * HEADS + h
                    if h == 0:
                        take(pe, ("atto", b))
                    o = bank(("atto", b))
                    pe.wait_ge(*brought(("pt", b, h)))
                    for j in range(b + 1):
                        mm = pe.matmul(o[:, h * DH:(h + 1) * DH], PTS[u % 2][:, j * P:(j + 1) * P],
                                       va[:, j, h * DH:(h + 1) * DH], start=(j == 0), stop=(j == b))
                    mm.then_inc(o_done, 1)

                def turn_o(b):
                    o = take(pe, ("attt", b))
                    pe.wait_ge(att_ready, b + 1)
                    for c in range(4):
                        mm = pe.transpose(o[:, c * P:(c + 1) * P], ATO[b % 2][:, c * P:(c + 1) * P], ident)
                    mm.then_inc(tp_done, 1)

                pe.wait_ge(*brought(("turn", "qa", NB - 1)))
                pe.wait_ge(v_ready, 2 * NB)
                heads = [(b, h) for b in range(NB) for h in range(HEADS)]
                for u in range(len(heads) + 4):
                    if u < len(heads):
                        scores(*heads[u])
                    if 2 <= u < len(heads) + 2:
                        turn_p(*heads[u - 2])
                    if 3 <= u < len(heads) + 3:
                        values(*heads[u - 3])
                    if u >= 4 and heads[u - 4][1] == HEADS - 1:
                        turn_o(heads[u - 4][0])

            def project():
                def wout(b):
                    if b == 0:
                        pe.wait_ge(*brought(("attt", NB - 1)))
                        land(pe, AT[("out", 0)])
                        land(pe, AT[("out", 1)])
                    take(pe, ("wout", b))
                    for n in range(2):
                        o = ps[plan.bank[("wout", b)] + n]
                        w = chunk(AT[("out", n)])
                        for k in range(KD):
                            mm = pe.matmul(o[:, :], hT3[:, k, b * P:(b + 1) * P], w[:, k, :], start=(k == 0),
                                           stop=(k == KD - 1))
                    mm.then_inc(wout_done, 1)

                def route(b):
                    pe.wait_ge(h2_ready, b + 1)
                    for q in range(2):
                        o = take(pe, ("h2", b, q))
                        v = H2[b % 2].rearrange("p (q k) -> p k q", k=KD)
                        for c in range(4):
                            mm = pe.transpose(o[:, c * P:(c + 1) * P], v[:, 4 * q + c, :], ident)
                        mm.then_inc(tp_done, 1)
                    pe.wait_ge(*brought(("h2", b, 1)))
                    if b == 0:
                        land(pe, AT[("router", 0)])
                        take(pe, ("router",))
                    w = chunk(AT[("router", 0)], NG + NE)
                    o = bank(("router",))
                    for k in range(KD):
                        mm = pe.matmul(o[:, b * 36:b * 36 + 36], H2T[b % 2][:, k, :], w[:, k, :], start=(k == 0),
                                       stop=(k == KD - 1))
                    mm.then_inc(router_done, 1)

                for b in range(NB + 1):
                    if b < NB:
                        wout(b)
                    if b >= 1:
                        route(b - 1)
                pe.wait_ge(oh_ready, 1)
                o = take(pe, ("rank",))
                for b in range(NB):
                    for q in range(b + 1):
                        pe.matmul(o[:, b * NE:(b + 1) * NE], cst[:, C_LT:C_LT + P] if q == b else ones,
                                  OH[:, q, :], start=(q == 0), stop=(q == b))
                for q in range(NB):
                    mm = pe.matmul(o[:, NB * NE:(NB + 1) * NE], ones, OH[:, q, :], start=(q == 0), stop=(q == NB - 1))
                mm.then_inc(rank_done, 1)

            for s in steps:
                if s[0] == "unit":
                    chunk_unit(*s[1:])
                elif s[0] == "turn":
                    turn(*s[1:])
                elif s[0] == "MOD":
                    mod(s[1])
                elif s[0] == "IDX":
                    idx()
                elif s[0] == "RET":
                    retention()
                elif s[0] == "RETT":
                    retention_turn()
                elif s[0] == "ATT":
                    attention()
                else:
                    project()

            def turn_x(e, par):
                pe.wait_ge(xg_in[par], 8 * (e - par) + 16)
                for q in range(2):
                    if not (isinstance(e, int) and e == 0):
                        pe.wait_ge(xt_ev, 2 * e - 1 + q)
                    v = XG[par].rearrange("p (q k) -> p k q", k=KD)
                    for c in range(4):
                        mm = pe.transpose(ps[2 + q][:, c * CAP:(c + 1) * CAP], v[:, 4 * q + c, :],
                                          cst[0:CAP, C_ID:C_ID + CAP])
                    mm.then_inc(xt_mm, 1)

            def gate_up(e, s):
                par = s % 2
                pe.wait_ge(landed[s], landed_by(e, s))
                pe.wait_ge(xt_ev, 2 * e + 2)
                if not (isinstance(e, int) and e < 2):
                    pe.wait_ge(hid_ready, e - 1)
                wg, wu, _ = expert(s)
                o = ps[4 + par]
                for m, w in enumerate((wg, wu)):
                    for i in range(KF):
                        c = (m * KF + i) * CAP
                        wv = w.rearrange("p k (q i) -> p k i q", i=KF)
                        for k in range(KD):
                            mm = pe.matmul(o[:, c:c + CAP], wv[:, k, i, :], XT[par][:, k, :], start=(k == 0),
                                           stop=(k == KD - 1))
                mm.then_inc(gu_mm, 1)

            def down(e, s):
                par = s % 2
                pe.wait_ge(hid_ready, e + 1)
                if not (isinstance(e, int) and e < 2):
                    pe.wait_ge(y_evA, e - 1)
                    pe.wait_ge(y_evV, e - 1)
                wd = expert(s)[2]
                for n in range(2):
                    o = ps[(0, 6)[par] + n]
                    for i in range(KF):
                        mm = pe.matmul(o[0:CAP, :], HID[par][:, i, :], wd[:, i, n * 512:(n + 1) * 512],
                                       start=(i == 0), stop=(i == KF - 1))
                    mm.then_inc(y_mm, 1)

            turn_x(0, 0)
            turn_x(1, 1)
            gate_up(0, 0)

            def experts(base, last):
                for j in range(RING):
                    e = base + j
                    if not (last and j == RING - 1):
                        gate_up(e + 1, (j + 1) % RING)
                    if not (last and j >= RING - 2):
                        turn_x(e + 2, j % 2)
                    down(e, j)

            experts(0, False)
            with pe.Fori(1, NE // RING - 1) as i:
                experts(i * RING, False)
            experts(NE - RING, True)

            def overflow(o):
                pe.wait_ge(ov_x, o * 16 + 16)
                rows = XG[0].rearrange("p (q k) -> p k q", k=KD)
                for k in range(KD):
                    mm = pe.transpose(ps[2 + k // 4][:, (k % 4) * CAP:(k % 4 + 1) * CAP], rows[:, k, :],
                                      cst[0:CAP, C_ID:C_ID + CAP])
                mm.then_inc(ov_turned, 1)
                pe.wait_ge(ov_brought, o + 1)
                pe.wait_ge(ov_w, o * 48 + 48)
                wg, wu, wd = expert(0)
                for m, w in enumerate((wg, wu)):
                    for i in range(KF):
                        c = (m * KF + i) * CAP
                        wv = w.rearrange("p k (q i) -> p k i q", i=KF)
                        for k in range(KD):
                            mm = pe.matmul(ps[4][:, c:c + CAP], wv[:, k, i, :], XT[0][:, k, :], start=(k == 0),
                                           stop=(k == KD - 1))
                mm.then_inc(ov_gu, 1)
                pe.wait_ge(ov_hid, o + 1)
                for n in range(2):
                    for i in range(KF):
                        mm = pe.matmul(ps[n][0:CAP, :], HID[0][:, i, :], wd[:, i, n * 512:(n + 1) * 512],
                                       start=(i == 0), stop=(i == KF - 1))
                mm.then_inc(ov_y, 1)
            pe.wait_ge(y_evA, NE)
            pe.wait_ge(y_evV, NE)
            each_overflow(pe, overflow)

        @block.scalar
        def _(act):
            a = nc.scalar
            act.dma_start(cc, t["c"].rearrange("a (p k) -> (a p) k", k=KD)).then_inc(params_in, 16)
            act.dma_start(posi[:, :], t["positions"].rearrange("a (b p) -> (a p) b", p=P),
                          allow_slow_non_contiguous=True).then_inc(params_in, 16)
            act.dma_start(cst[:, :], t["cst"]).then_inc(params_in, 16)
            act.dma_start(cg, pcol("g_pre_mix")).then_inc(params_in, 16)
            act.dma_start(cb.rearrange("p (m k) -> p m k", m=2),
                          b_ada[0:2, :].rearrange("m (p k) -> p m k", k=KD)).then_inc(params_in, 16)
            act.dma_start(G1[:, :], prow(t["g_post_mix"], D)).then_inc(params_in, 16)
            act.dma_start(S2[:, :], prow(t["g_pre_ffn"], D)).then_inc(params_in, 16)
            act.dma_start(rb[:, 0:NG], prow(t["b_group"], NG)).then_inc(params_in, 16)
            act.dma_start(rb[:, NG:NG + NE], prow(t["b_expert"], NE)).then_inc(params_in, 16)
            act.dma_start(pairc[:, :], t["pair"]).then_inc(params_in, 16)
            act.wait_ge(params_in, PARAMS)
            a.activation(ctmp[:, 0:8], cc, ACT.Exp, scale=-1.0).then_inc(c_exp, 1)
            act.wait_ge(ang_ready, 1)
            a.activation(sinT[:, :], sinT[:, :], ACT.Sin).then_inc(trig_ready, 1)
            a.activation(cosT[:, :], cosT[:, :], ACT.Sin).then_inc(trig_ready, 1)
            act.wait_ge(x_in, 16)
            for b in range(NB):
                a.activation(xn[:, b, :], x3[:, b, :], ACT.Square, accum_out=ss1[:, b:b + 1]).then_inc(x_ss, 1)
            act.wait_ge(x_ss, NB)
            a.activation(r1, ss1, ACT.Sqrt, bias=eps, scale=1.0 / D).then_inc(x_sq, 1)

            def bring(use, dst):
                act.wait_ge(tp_done, plan.tp[use] + 1)
                n = dst.shape[1] if len(dst.shape) == 2 else dst.shape[1] * dst.shape[2]
                src = bank(use)[:, 0:n]
                if len(dst.shape) == 3:
                    src = src.rearrange("p (c t) -> p c t", c=dst.shape[1])
                a.activation(dst, src, ACT.Copy).then_inc(evac, 1)

            act.wait_ge(gs_ready, 2)
            for k in range(KD):
                act.wait_ge(tp_done, k + 1)
                a.activation(hT3[:, k, :], bank(("x", k))[:, :], ACT.Identity, bias=sh1[:, k:k + 1],
                             scale=gs1[:, k:k + 1]).then_inc(evac, 1)

            into = {"qi": qiT, "qr": qrT, "kr": krT, "ka": kaT, "qa": qaT}
            for s in steps:
                if s in plan.v:
                    name, b = s[1:]
                    act.wait_ge(unit_done, plan.unit[s] + 1)
                    a.activation((vr if name == "vr" else va)[:, b, :], bank(s)[:, :], ACT.Copy).then_inc(v_ready, 1)
                elif s[0] == "unit" and s[1] == "gr":
                    act.wait_ge(unit_done, plan.unit[s] + 1)
                    a.activation(gr[:, s[2], :], bank(s)[:, :], ACT.Exp, scale=-1.0).then_inc(g_exp, 1)
                elif s[0] == "turn":
                    name, b = s[1:]
                    if name == "kw":
                        bring(s, kiT[:, b * P:(b + 1) * P])
                    else:
                        if (name, b) == ("qa", 0):
                            act.wait_ge(it_ready, NB * RHEADS)
                        bring(s, into[name][:, :, b * P:(b + 1) * P])
                elif s[0] == "IDX":
                    for u in range((NB - 1) * HEADS):
                        b, h = u // HEADS + 1, u % HEADS
                        n = (b + 1) * P
                        act.wait_ge(sc_done, u + 1)
                        if u >= 2:
                            act.wait_ge(relu_used, u - 1)
                        a.activation(RELU[u % 2][:, 0:n], bank(("idx", b, h))[:, 0:n], ACT.Relu).then_inc(relu_ready, 1)
                elif s[0] == "RET":
                    act.wait_ge(sc_done, (NB - 1) * HEADS)
                    for h in range(RHEADS):
                        act.wait_ge(o_done, h + 1)
                        a.activation(Rsb[:, :, h * RDH:(h + 1) * RDH],
                                     bank(("reto", h))[:, :].rearrange("p (b e) -> p b e", b=NB),
                                     ACT.Copy).then_inc(R_ready, 1)
                    act.wait_ge(ret_ss, 1)
                    a.activation(rr, ssr, ACT.Sqrt, bias=eps, scale=1.0 / RDH).then_inc(ret_sq, 1)
                elif s[0] == "RETT":
                    act.wait_ge(unit_done, len(plan.unit))
                    for b in range(NB):
                        bring(("rett", b), hT3[:, 4:8, b * P:(b + 1) * P])
                elif s[0] == "ATT":
                    for u in range(len(AHEADS) + 4):
                        if u < len(AHEADS):
                            b, h = AHEADS[u]
                            n = (b + 1) * P
                            act.wait_ge(att_max, u + 1)
                            if u >= 2:
                                act.wait_ge(tp_done, plan.tp[("pt",) + AHEADS[u - 2]] + 1)
                            a.activation(PEX[u % 2][:, 0:n], SMX[u % 2][:, 0:n], ACT.Exp, bias=nmx[:, u % 2:u % 2 + 1],
                                         scale=-1.0, accum_out=rsum[:, b, h:h + 1]).then_inc(att_exp, 1)
                        if 2 <= u < len(AHEADS) + 2:
                            b, h = AHEADS[u - 2]
                            if u >= 4:
                                act.wait_ge(o_done, RHEADS + u - 3)
                            bring(("pt", b, h), PTS[u % 2][:, 0:(b + 1) * P])
                        if u >= 4 and AHEADS[u - 4][1] == HEADS - 1:
                            b = AHEADS[u - 4][0]
                            bring(("attt", b), hT3[:, 0:4, b * P:(b + 1) * P])
                    act.dma_start(G2, prow(t["g_post_ffn"], D)).then_inc(g2_in, 16)
                elif s[0] == "OUT":
                    for b in range(NB + 1):
                        if b < NB:
                            w = plan.bank[("wout", b)] * 512
                            act.wait_ge(wout_done, b + 1)
                            a.activation(JUNK, psum[:, w:w + D], ACT.Square, accum_out=ssm[:, b:b + 1]).then_inc(mix_ss, 1)
                            act.wait_ge(mix_ss, b + 1)
                            a.activation(rm[:, b:b + 1], ssm[:, b:b + 1], ACT.Sqrt, bias=eps,
                                         scale=1.0 / D).then_inc(mix_sq, 1)
                            act.wait_ge(res_ready, b + 1)
                            a.activation(JUNK, x3[:, b, :], ACT.Square, accum_out=ss2[:, b:b + 1]).then_inc(res_ss, 1)
                            act.wait_ge(res_ss, b + 1)
                            a.activation(r2[:, b:b + 1], ss2[:, b:b + 1], ACT.Sqrt, bias=eps,
                                         scale=1.0 / D).then_inc(res_sq, 1)
                        if b >= 1:
                            if b >= 3:
                                act.wait_ge(router_done, b - 2)
                            for q in range(2):
                                bring(("h2", b - 1, q), H2T[(b - 1) % 2][:, 4 * q:4 * q + 4, :])
                    act.wait_ge(g_sub, 1)
                    a.activation(GEXV, GSUBV, ACT.Exp).then_inc(g_exped, 1)
                    act.wait_ge(d_sub, 1)
                    a.activation(P2, DSUB, ACT.Exp).then_inc(d_exped, 1)

            def turned(e, par):
                if not (isinstance(e, int) and e < 2):
                    act.wait_ge(gu_mm, e - 1)
                for q in range(2):
                    act.wait_ge(xt_mm, 2 * e + 1 + q)
                    a.activation(XT[par][:, 4 * q:4 * q + 4, :],
                                 ps[2 + q][:, 0:4 * CAP].rearrange("p (k c) -> p k c", k=4), ACT.Copy).then_inc(xt_ev, 1)

            def gated(e, par):
                act.wait_ge(gu_mm, e + 1)
                if not (isinstance(e, int) and e < 2):
                    act.wait_ge(hid_ready, e - 1)
                a.activation(EG[par], ps[4 + par][:, 0:W2], ACT.Exp, scale=-1.0).then_inc(gu_exp, 1)

            def downed(e, par):
                act.wait_ge(y_mm, 2 * e + 1)
                if not (isinstance(e, int) and e < 2):
                    act.wait_ge(y_out[par], 8 * (e - par))
                a.activation(YO[par][:, 0:512], ps[(0, 6)[par]][0:CAP, :], ACT.Copy).then_inc(y_evA, 1)

            turned(0, 0)
            turned(1, 1)
            gated(0, 0)

            def experts(base, last):
                for j in range(RING):
                    e = base + j
                    if not (last and j == RING - 1):
                        gated(e + 1, (j + 1) % 2)
                    if not (last and j >= RING - 2):
                        turned(e + 2, j % 2)
                    downed(e, j % 2)

            experts(0, False)
            with act.Fori(1, NE // RING - 1) as i:
                experts(i * RING, False)
            experts(NE - RING, True)

            def overflow(o):
                act.wait_ge(ov_turned, o + 1)
                for q in range(2):
                    ins = a.activation(XT[0][:, 4 * q:4 * q + 4, :],
                                       ps[2 + q][:, 0:4 * CAP].rearrange("p (k c) -> p k c", k=4), ACT.Copy)
                ins.then_inc(ov_brought, 1)
                act.wait_ge(ov_gu, o + 1)
                a.activation(EG[0], ps[4][:, 0:W2], ACT.Exp, scale=-1.0).then_inc(ov_exp, 1)
                act.wait_ge(ov_y, o + 1)
                a.activation(YO[0][:, 0:512], ps[0][0:CAP, :], ACT.Copy).then_inc(ov_evA, 1)
            act.wait_ge(y_out[0], 8 * NE)
            each_overflow(act, overflow)

            act.wait_ge(y_base, 1)
            rows = y_dram.rearrange("(b p j) d -> b p j d", b=NB, j=2)
            act.dma_start(YG[0], rows[0]).then_inc(y_back[0], 16)
            act.dma_start(YG[1], rows[1]).then_inc(y_back[1], 16)
            for b in range(NB):
                act.wait_ge(yw_ready, b + 1)
                a.activation(JUNK2, YG[b % 2][:, 0, :], ACT.Square, accum_out=yss[:, b:b + 1]).then_inc(y_ss, 1)
                act.wait_ge(y_ss, b + 1)
                a.activation(yr[:, b:b + 1], yss[:, b:b + 1], ACT.Sqrt, bias=eps, scale=1.0 / D).then_inc(y_sq, 1)
                if b + 2 < NB:
                    act.wait_ge(o_out[b % 2], 16 * (b // 2 + 1))
                    act.dma_start(YG[b % 2], rows[b + 2]).then_inc(y_back[b % 2], 16)

        @block.vector
        def _(dve):
            v = nc.vector
            chained = [0]

            def link(ins):
                chained[0] += 1
                ins.then_inc(v_chain, 1)
                dve.wait_ge(v_chain, chained[0])

            def relay(ins, s, n):
                ins.then_inc(s, 1)
                dve.wait_ge(s, n)

            v.memset(pid_t[:, :], NOBODY).then_inc(nobody_set, 1)
            dve.wait_ge(params_in, PARAMS)
            link(v.tensor_copy(posf, posi[:, :]))
            for b in range(NB):
                last = v.tensor_scalar(sinT[:, b * 64:(b + 1) * 64], cst[:, C_FREQ:C_FREQ + 64], posf[:, b:b + 1], None,
                                       ALU.mult)
            link(last)
            link(v.tensor_scalar(cosT[:, :], sinT[:, :], 1.0 / (2 * math.pi), MAGIC, ALU.mult, ALU.add))
            link(v.tensor_scalar(cosT[:, :], cosT[:, :], MAGIC, None, ALU.subtract))
            for part in TWO_PI:
                link(v.scalar_tensor_tensor(out=sinT[:, :], in0=cosT[:, :], scalar=-part, in1=sinT[:, :], op0=ALU.mult,
                                            op1=ALU.add))
            link(v.tensor_scalar(sinT[:, :], sinT[:, :], 3.1415925, -3.1415925, ALU.min, ALU.max))
            link(v.scalar_tensor_tensor(out=cosT[:, :], in0=sinT[:, :], scalar=-1.0, in1=sinT[:, :], op0=ALU.mult,
                                        op1=ALU.min))
            v.tensor_scalar(cosT[:, :], cosT[:, :], math.pi / 2, None, ALU.add).then_inc(ang_ready, 1)
            dve.wait_ge(c_exp, 1)
            link(v.tensor_scalar(ctmp[:, 8:16], ctmp[:, 0:8], 1.0, None, ALU.add))
            link(v.reciprocal(ctmp[:, 0:8], ctmp[:, 8:16]))
            link(v.tensor_tensor(sc_, cc, ctmp[:, 0:8], ALU.mult))
            dve.wait_ge(x_sq, 1)
            link(v.reciprocal(ss1, r1))
            for b in range(NB):
                v.tensor_scalar(xn[:, b, :], x3[:, b, :], ss1[:, b:b + 1], None, ALU.mult).then_inc(x_n, 1)

            def ada(i):
                m, half = i // 2, i % 2
                land(dve, AT[("ada", i)])
                acc = (accA[:, m, :] if m < 2 else accB[:, :])[:, half * 512:(half + 1) * 512]
                w = chunk(AT[("ada", i)])
                if m >= 2 and half == 0:
                    if m > 2:
                        dve.wait_ge(mod_done, 2 * (m - 2))
                    v.memset(accB[:, :], 0.0).then_inc(accB_clear, 1)
                    dve.wait_ge(bias_in, 16 * (m - 1))
                if m < 2:
                    link(v.tensor_scalar(acc, w[:, 0, :], sc_[:, 0:1], None, ALU.mult))
                for k in range(1 if m < 2 else 0, KD):
                    ins = v.scalar_tensor_tensor(out=acc, in0=w[:, k, :], scalar=sc_[:, k:k + 1], in1=acc, op0=ALU.mult,
                                                 op1=ALU.add)
                    if k < KD - 1:
                        link(ins)
                ins.then_inc(ada_done, 1)

            for i in range(4):
                ada(i)
            dve.wait_ge(modA_done, 1)
            o = bank(("modA",))
            v.tensor_tensor(sh1, o[:, 0:KD], cb[:, 0:KD], ALU.add).then_inc(gs_ready, 1)
            link(v.tensor_tensor(modA_s[:, 0:KD], o[:, KD:2 * KD], cb[:, KD:2 * KD], ALU.add))
            v.scalar_tensor_tensor(out=gs1, in0=modA_s[:, 0:KD], scalar=1.0, in1=cg, op0=ALU.add,
                                   op1=ALU.mult).then_inc(gs_ready, 1)

            def rotate(s):
                name, b = s[1:]
                r, d = plan.rope[s], ROPE[name]
                width = 64 if name == "kw" else 512
                heads, hd = width // d, d // 2
                dve.wait_ge(unit_done, plan.unit[s] + 1)
                if r == 0:
                    dve.wait_ge(trig_ready, 2)
                else:
                    dve.wait_ge(roped, r)
                src = bank(s)[:, 0:width].rearrange("p (h a i) -> p h a i", h=heads, a=2)
                for n, tab in enumerate((cosT, sinT)):
                    tb = tab[:, b * 64:(b + 1) * 64].rearrange("p (i e) -> p i e", e=64 // hd)[:, :, 0]
                    tb = tb.unsqueeze(1).unsqueeze(1).to_broadcast([P, heads, 2, hd])
                    dst = ropebuf[:, n * 512:n * 512 + width].rearrange("p (h a i) -> p h a i", h=heads, a=2)
                    if n == 1 and name == "kw":
                        v.tensor_scalar(wi[:, b, :], bank(s)[:, DH:KW], IDX_SCALE, None, ALU.mult)
                    ins = v.tensor_tensor(dst, src, tb, ALU.mult)
                ins.then_inc(rope_ab, 1)

            def mask_of(b):
                at = (None, 0, 256, 640)[b]
                return cst[:, C_CAUSAL:C_CAUSAL + P] if b == 0 else score[:, at:at + (b + 1) * P]

            def topk():
                for b in range(1, NB):
                    m = mask_of(b)
                    for r in range(TOPK // 8):
                        link(v.max(top8, m))
                        link(v.match_replace(m, top8, m, TAKEN))
                        if r == TOPK // 8 - 1:
                            link(v.tensor_scalar(m, m, TAKEN / 2, NEG, ALU.is_gt, ALU.mult))
                        yield

            rounds = topk()

            def select_keys(n):
                for _ in range(n):
                    next(rounds, None)

            def first_best(x, best, marks, least, numbers, n, chosen):
                link(v.tensor_reduce(best.rearrange("p b n -> p (b n)"), x, AX, ALU.max))
                link(v.tensor_tensor(marks, x, best.to_broadcast([P, NB, n]), ALU.is_equal))
                link(v.scalar_tensor_tensor(out=marks, in0=numbers, scalar=float(-n), in1=marks, op0=ALU.add,
                                            op1=ALU.mult))
                link(v.tensor_reduce(least.rearrange("p b n -> p (b n)"), marks, AX, ALU.min))
                link(v.tensor_tensor(chosen, marks, least.to_broadcast([P, NB, n]), ALU.is_equal))

            def routing():
                def numbers(n):
                    return cst[:, C_EIDX:C_EIDX + n].unsqueeze(1).to_broadcast([P, NB, n])

                def flat(x):
                    return x.rearrange("p b n -> p (b n)")

                dve.wait_ge(router_done, NB)
                relay(v.tensor_tensor(LG, bank(("router",))[:, 0:144].rearrange("p (b n) -> p b n", b=NB),
                                      rb[:, :].unsqueeze(1).to_broadcast([P, NB, NG + NE]), ALU.add), lg_ready, 1)
                first_best(LG[:, :, 0:NG], GMAX, GT, GM, numbers(NG), NG, SG)
                v.tensor_tensor(GSUBV, LG[:, :, 0:NG], GMAX.to_broadcast([P, NB, NG]), ALU.subtract).then_inc(g_sub, 1)
                prod = retbuf[:, 384:512].rearrange("p (b e g) -> p b e g", b=NB, e=EPG)
                for b in range(NB):
                    last = v.tensor_tensor(prod[:, b, :, :], LG[:, b, NG:].rearrange("p (g e) -> p e g", g=NG),
                                           SG[:, b, :].unsqueeze(1).to_broadcast([P, EPG, NG]), ALU.mult)
                link(last)
                link(v.tensor_reduce(flat(EL), retbuf[:, 384:512].rearrange("p (q g) -> p q g", g=NG), AX, ALU.add))
                first_best(EL, EMAX, ET, EM, numbers(EPG), EPG, O1)
                link(v.scalar_tensor_tensor(out=EL2, in0=O1, scalar=NEG, in1=EL, op0=ALU.mult, op1=ALU.add))
                first_best(EL2, EMAX2, ET, EM, numbers(EPG), EPG, O2)
                v.tensor_tensor(flat(DSUB), flat(EMAX2), flat(EMAX), ALU.subtract).then_inc(d_sub, 1)
                for b in range(NB):
                    for oh, o in ((OH1, O1), (OH2, O2)):
                        last = v.tensor_tensor(oh[:, b, :].rearrange("p (g e) -> p g e", g=NG),
                                               SG[:, b, :].unsqueeze(2).to_broadcast([P, NG, EPG]),
                                               o[:, b, :].unsqueeze(1).to_broadcast([P, NG, EPG]), ALU.mult)
                link(last)
                v.tensor_tensor(OH, OH1, OH2, ALU.add).then_inc(oh_ready, 1)
                dve.wait_ge(g_exped, 1)
                link(v.tensor_reduce(flat(GSUM), GEXV, AX, ALU.add))
                link(v.reciprocal(flat(GTOP), flat(GSUM)))
                dve.wait_ge(d_exped, 1)
                link(v.tensor_scalar(flat(WT), flat(P2), 1.0, None, ALU.add))
                link(v.reciprocal(flat(DSUB), flat(WT)))
                link(v.tensor_tensor(wts[:, :, 0:1], DSUB, GTOP, ALU.mult))
                v.tensor_tensor(wts[:, :, 1:2], wts[:, :, 0:1], P2, ALU.mult)
                dve.wait_ge(rank_done, 1)
                o = bank(("rank",))
                v.tensor_copy(flat(RANK), o[:, 0:NB * NE])
                link(v.tensor_copy(CNT, o[:, NB * NE:(NB + 1) * NE]))
                link(v.tensor_scalar(MFL, RANK, float(CAP), None, ALU.is_ge))
                link(v.tensor_scalar(OV, CNT, float(CAP), None, ALU.is_gt))
                for m in range(2, NM):
                    v.scalar_tensor_tensor(out=MFL, in0=RANK, scalar=float(m * CAP), in1=MFL, op0=ALU.is_ge,
                                           op1=ALU.add).then_inc(v_chain, 1)
                    v.scalar_tensor_tensor(out=OV, in0=CNT, scalar=float(m * CAP), in1=OV, op0=ALU.is_gt,
                                           op1=ALU.add).then_inc(v_chain, 1)
                    chained[0] += 2
                    dve.wait_ge(v_chain, chained[0])
                link(v.tensor_tensor_scan(BINC, ones[:, 0:NE], OV, 0.0, ALU.mult, ALU.add))
                v.tensor_tensor(OVC, BINC.unsqueeze(1).to_broadcast([P, NOV, NE]),
                                cst[:, C_OIDX:C_OIDX + NOV].unsqueeze(2).to_broadcast([P, NOV, NE]), ALU.is_le)
                link(v.tensor_tensor(BEX, BINC, OV, ALU.subtract))
                link(v.tensor_tensor(BEX, BEX, cst[:, C_EIDX:C_EIDX + NE], ALU.subtract))
                link(v.tensor_reduce(EO, OVC, AX, ALU.add))
                link(v.tensor_scalar(EO, EO, float(NE - 1), None, ALU.min))
                v.tensor_copy(ctl[:, 0:NOV], EO)
                v.tensor_copy(ctl[:, NOV:NOV + 1], BINC[:, NE - 1:NE]).then_inc(ctl_ready, 1)
                link(v.scalar_tensor_tensor(out=QT, in0=MFL, scalar=float(NE - 1),
                                            in1=BEX.unsqueeze(1).to_broadcast([P, NB, NE]), op0=ALU.add, op1=ALU.add))
                link(v.scalar_tensor_tensor(out=QT, in0=MFL, scalar=0.0, in1=QT, op0=ALU.is_gt, op1=ALU.mult))
                link(v.tensor_tensor(QT, QT, numbers(NE), ALU.add))
                link(v.scalar_tensor_tensor(out=MFL, in0=MFL, scalar=float(-CAP), in1=RANK, op0=ALU.mult,
                                            op1=ALU.add))
                link(v.scalar_tensor_tensor(out=ADR, in0=MFL, scalar=float(NT), in1=QT, op0=ALU.mult, op1=ALU.add))
                for j, oh in enumerate((OH1, OH2)):
                    link(v.tensor_tensor(TMP, oh, ADR, ALU.mult))
                    link(v.tensor_reduce(POS[:, :, j], TMP, AX, ALU.add))
                v.tensor_copy(addr_i[:, :], retbuf[:, 1728:1736]).then_inc(addr_ready, 1)
                dve.wait_ge(tab_in, 16)
                v.tensor_scalar(tok_t[0:CAP, :], pid_t[0:CAP, :], 1, None, ALU.logical_shift_right).then_inc(tok_ready, 1)

            for s in steps:
                if s in plan.rope:
                    rotate(s)
                    if s[1] in ("kr", "ka", "qa"):
                        select_keys(2)
                elif s in plan.v:
                    select_keys(2)
                elif s[0] == "unit":
                    b = s[2]
                    dve.wait_ge(g_exp, b + 1)
                    link(v.tensor_scalar(gr[:, b, :], gr[:, b, :], 1.0, None, ALU.add))
                    link(v.reciprocal(gr[:, b, :], gr[:, b, :]))
                    v.tensor_tensor(gr[:, b, :], bank(s)[:, :], gr[:, b, :], ALU.mult).then_inc(g_ready, 1)
                    select_keys(2)
                elif s[0] == "IDX":
                    for u in range((NB - 1) * HEADS):
                        b, h = u // HEADS + 1, u % HEADS
                        m, n = mask_of(b), (b + 1) * P
                        dve.wait_ge(relu_ready, u + 1)
                        r = RELU[u % 2][:, 0:n]
                        if h == 0:
                            relay(v.tensor_scalar(m, r, wi[:, b, h:h + 1], None, ALU.mult), relu_used, u + 1)
                        else:
                            relay(v.scalar_tensor_tensor(out=m, in0=r, scalar=wi[:, b, h:h + 1], in1=m, op0=ALU.mult,
                                                         op1=ALU.add), relu_used, u + 1)
                        if h == HEADS - 1:
                            link(v.tensor_tensor(m[:, b * P:n], m[:, b * P:n], cst[:, C_CAUSAL:C_CAUSAL + P], ALU.add))
                elif s[0] == "RET":
                    dve.wait_ge(decay_in, 16)
                    for h in range(RHEADS):
                        if h >= 2:
                            dve.wait_ge(o_done, h - 1)
                        for j in range(NB):
                            n = S - j * P
                            dve.wait_ge(sc_done, plan.sc[("ret", h, j)] + 1)
                            v.tensor_tensor(iT(h, j), bank(("ret", h, j))[:, 0:n], decay[:, h, 0:n],
                                            ALU.mult).then_inc(it_ready, 1)
                    dve.wait_ge(R_ready, RHEADS)
                    sq = retbuf[:, 0:2048]
                    flat = work[:, 6144:8192]
                    link(v.tensor_tensor(sq, flat, flat, ALU.mult))
                    v.tensor_reduce(ssr, sq.rearrange("p (g e) -> p g e", g=16), AX, ALU.add).then_inc(ret_ss, 1)
                    dve.wait_ge(ret_sq, 1)
                    link(v.reciprocal(ssr, rr))
                    for b in range(NB):
                        for h in range(RHEADS):
                            e = slice(h * RDH, (h + 1) * RDH)
                            ins = v.scalar_tensor_tensor(out=Rsb[:, b, e], in0=Rsb[:, b, e],
                                                         scalar=ssr[:, b * 4 + h:b * 4 + h + 1], in1=gr[:, b, e],
                                                         op0=ALU.mult, op1=ALU.mult)
                        ins.then_inc(ret_ready, 1)
                elif s[0] == "MOD":
                    m = s[1]
                    dve.wait_ge(mod_done, 2 * (m - 2) + 2)
                    for n in range(2):
                        c = slice(n * 512, (n + 1) * 512)
                        o = bank(("MOD", m, n))
                        if m == 2:
                            ins = v.tensor_tensor(G1[:, c], o, G1[:, c], ALU.mult)
                        elif m == 3:
                            ins = v.tensor_copy(T2[:, c], o)
                        elif m == 4:
                            ins = v.scalar_tensor_tensor(out=S2[:, c], in0=o, scalar=1.0, in1=S2[:, c], op0=ALU.add,
                                                         op1=ALU.mult)
                        else:
                            dve.wait_ge(g2_in, 16)
                            ins = v.tensor_tensor(G2[:, c], o, G2[:, c], ALU.mult)
                        ins.then_inc(mod_ready, 1)
                elif s[0] == "ATT":
                    select_keys(1000)
                    for u in range(len(AHEADS) + 4):
                        if u < len(AHEADS):
                            b, h = AHEADS[u]
                            n = (b + 1) * P
                            dve.wait_ge(sc_done, plan.sc[("att", b, h)] + 1)
                            if u >= 2:
                                dve.wait_ge(att_exp, u - 1)
                            v.tensor_tensor_reduce(SMX[u % 2][:, 0:n], bank(("att", b, h))[:, 0:n], mask_of(b),
                                                   -ATT_SCALE, 3.0e38, ALU.add, ALU.min,
                                                   nmx[:, u % 2:u % 2 + 1]).then_inc(att_max, 1)
                        if u >= 4 and AHEADS[u - 4][1] == HEADS - 1:
                            b = AHEADS[u - 4][0]
                            dve.wait_ge(att_exp, u - 3)
                            link(v.reciprocal(rinv, rsum[:, b, :]))
                            dve.wait_ge(o_done, RHEADS + u - 3)
                            if b >= 2:
                                dve.wait_ge(tp_done, plan.tp[("attt", b - 2)] + 1)
                            v.tensor_tensor(ATO[b % 2].rearrange("p (h e) -> p h e", h=HEADS),
                                            bank(("atto", b))[:, :].rearrange("p (h e) -> p h e", h=HEADS),
                                            rinv.unsqueeze(2).to_broadcast([P, HEADS, DH]),
                                            ALU.mult).then_inc(att_ready, 1)
                elif s[0] == "OUT":
                    for b in range(NB):
                        w = plan.bank[("wout", b)] * 512
                        dve.wait_ge(mix_sq, b + 1)
                        link(v.reciprocal(ssm[:, b:b + 1], rm[:, b:b + 1]))
                        if b >= 2:
                            dve.wait_ge(res_ready, b - 1)
                        if b == 0:
                            dve.wait_ge(mod_ready, 8)
                        v.scalar_tensor_tensor(out=MIXN[b % 2], in0=psum[:, w:w + D], scalar=ssm[:, b:b + 1],
                                               in1=G1[:, :], op0=ALU.mult, op1=ALU.mult).then_inc(mix_n, 1)
                        dve.wait_ge(res_sq, b + 1)
                        link(v.reciprocal(ss2[:, b:b + 1], r2[:, b:b + 1]))
                        if b >= 2:
                            dve.wait_ge(tp_done, plan.tp[("h2", b - 2, 1)] + 1)
                            dve.wait_ge(h2_out[b % 2], 16)
                        v.scalar_tensor_tensor(out=H2[b % 2], in0=x3[:, b, :], scalar=ss2[:, b:b + 1], in1=S2[:, :],
                                               op0=ALU.mult, op1=ALU.mult).then_inc(h2_a, 1)
                    routing()
                if s[0] == "unit" and s[2] == NB - 1:
                    n = AT[("in", s[1])] + 1
                    while ITEMS[n][0] == "ada":
                        ada(ITEMS[n][1])
                        n += 1

            def gate(e, par):
                dve.wait_ge(gu_exp, e + 1)
                g = ps[4 + par]
                v.tensor_scalar(EG[par], EG[par], 1.0, None, ALU.add).then_inc(gu_step, 1)
                dve.wait_ge(gu_step, 3 * e + 1)
                v.reciprocal(EG[par], EG[par]).then_inc(gu_step, 1)
                dve.wait_ge(gu_step, 3 * e + 2)
                v.tensor_tensor(EG[par], g[:, 0:W2], EG[par], ALU.mult).then_inc(gu_step, 1)
                dve.wait_ge(gu_step, 3 * e + 3)
                v.tensor_tensor(HID[par].rearrange("p i c -> p (i c)"), g[:, W2:2 * W2], EG[par],
                                ALU.mult).then_inc(hid_ready, 1)

            def downed(e, par):
                dve.wait_ge(y_mm, 2 * e + 2)
                if not (isinstance(e, int) and e < 2):
                    dve.wait_ge(y_out[par], 8 * (e - par))
                v.tensor_copy(YO[par][:, 512:1024], ps[(0, 6)[par] + 1][0:CAP, :]).then_inc(y_evV, 1)

            gate(0, 0)

            def experts(base, last):
                for j in range(RING):
                    if not (last and j == RING - 1):
                        gate(base + (j + 1), (j + 1) % 2)
                    downed(base + j, j % 2)

            experts(0, False)
            with dve.Fori(1, NE // RING - 1) as i:
                experts(i * RING, False)
            experts(NE - RING, True)

            def overflow(o):
                dve.wait_ge(ov_exp, o + 1)
                v.tensor_scalar(EG[0], EG[0], 1.0, None, ALU.add).then_inc(ov_step, 1)
                dve.wait_ge(ov_step, o * 3 + 1)
                v.reciprocal(EG[0], EG[0]).then_inc(ov_step, 1)
                dve.wait_ge(ov_step, o * 3 + 2)
                v.tensor_tensor(EG[0], ps[4][:, 0:W2], EG[0], ALU.mult).then_inc(ov_step, 1)
                dve.wait_ge(ov_step, o * 3 + 3)
                v.tensor_tensor(HID[0].rearrange("p i c -> p (i c)"), ps[4][:, W2:2 * W2], EG[0],
                                ALU.mult).then_inc(ov_hid, 1)
                dve.wait_ge(ov_y, o + 1)
                v.tensor_copy(YO[0][:, 512:1024], ps[1][0:CAP, :]).then_inc(ov_evV, 1)
            dve.wait_ge(y_out[0], 8 * NE)
            each_overflow(dve, overflow)

            for b in range(NB):
                y = YG[b % 2]
                dve.wait_ge(y_back[b % 2], 16 * (b // 2 + 1))
                link(v.tensor_scalar(y[:, 1, :], y[:, 1, :], wts[:, b, 1:2], None, ALU.mult))
                relay(v.scalar_tensor_tensor(out=y[:, 0, :], in0=y[:, 0, :], scalar=wts[:, b, 0:1], in1=y[:, 1, :],
                                             op0=ALU.mult, op1=ALU.add), yw_ready, b + 1)
                dve.wait_ge(y_sq, b + 1)
                link(v.reciprocal(yss[:, b:b + 1], yr[:, b:b + 1]))
                v.scalar_tensor_tensor(out=y[:, 1, :], in0=y[:, 0, :], scalar=yss[:, b:b + 1], in1=G2,
                                       op0=ALU.mult, op1=ALU.mult).then_inc(o_mul, 1)

        @block.gpsimd
        def _(pool):
            g = nc.gpsimd
            pool.wait_ge(nobody_set, 1)
            pool.dma_start(tab_rows, pid_t[0:CAP, :]).then_inc(tab_init, 16)

            def rotate(s):
                name, b = s[1:]
                r, d = plan.rope[s], ROPE[name]
                width = 64 if name == "kw" else 512
                heads = width // d
                at = 1024 + (r % 2) * 512
                pool.wait_ge(rope_ab, r + 1)
                if r >= 2:
                    pool.wait_ge(tp_done, plan.tp[turns[r - 2]] + 1)
                xc, xs_ = (ropebuf[:, n * 512:n * 512 + width].rearrange("p (h a i) -> p h a i", h=heads, a=2)
                           for n in range(2))
                for copy in range(2 if name == "kw" else 1):
                    dst = ropebuf[:, at + copy * 64:at + copy * 64 + width].rearrange("p (h a i) -> p h a i", h=heads,
                                                                                      a=2)
                    g.tensor_tensor(dst[:, :, 0, :], xc[:, :, 0, :], xs_[:, :, 1, :], ALU.subtract)
                    ins = g.tensor_tensor(dst[:, :, 1, :], xc[:, :, 1, :], xs_[:, :, 0, :], ALU.add)
                ins.then_inc(roped, 1)

            turns = [("turn",) + s[1:] for s in plan.rope]
            for s in steps:
                if s in plan.rope:
                    rotate(s)
                if s[0] == "unit" and s[2] == NB - 1:
                    kind, i = ITEMS[AT[("in", s[1])] + 1]
                    if kind == "ada" and i % 2 == 0:
                        m = i // 2
                        pool.wait_ge(accB_clear, m - 1)
                        pool.dma_start(accB[0:1, :], b_ada[m:m + 1, :]).then_inc(bias_in, 16)
            for b in range(NB):
                pool.wait_ge(mix_n, b + 1)
                g.tensor_tensor(x3[:, b, :], x3[:, b, :], MIXN[b % 2], ALU.add).then_inc(res_ready, 1)
                pool.wait_ge(h2_a, b + 1)
                g.tensor_tensor(H2[b % 2], H2[b % 2], T2[:, :], ALU.add).then_inc(h2_ready, 1)
                pool.wait_ge(h2_ready, b + 1)
                pool.dma_start(h2_dram[b * P:(b + 1) * P, :], H2[b % 2]).then_inc(h2_out[b % 2], 16)
            pool.wait_ge(tab_init, 16)
            pool.wait_ge(addr_ready, 1)
            for n in range(2 * NB):
                g.indirect_dma_start(out=tab_dram, out_offset=bass.IndirectOffsetOnAxis(ap=addr_i[:, n:n + 1], axis=0),
                                     in_=pairc[:, n:n + 1], in_offset=None).then_inc(tab_set, 16)
            pool.wait_ge(tab_set, 16 * 2 * NB)
            pool.dma_start(pid_t[0:CAP, :], tab_rows).then_inc(tab_in, 16)
            pool.wait_ge(h2_out[0], 16 * (NB // 2))
            pool.wait_ge(h2_out[1], 16 * (NB // 2))
            pool.wait_ge(tok_ready, 1)

            token_bound, pair_bound = g.to_reg(S - 1), g.to_reg(2 * S - 1)

            def gather(e, par):
                if not (isinstance(e, int) and e < 2):
                    pool.wait_ge(xt_mm, 2 * e - 2)
                    pool.wait_ge(xg_in[par], 8 * (e - par))
                g.tensor_copy(gix[0:CAP, par:par + 1], col(tok_t, e)).then_inc(ix_ready, 1)
                pool.wait_ge(ix_ready, e + 1 if isinstance(e, int) and e < 2 else 2 * e - 1)
                pool.sem_inc(pool_steps, 1)
                g.indirect_dma_start(out=XG[par], out_offset=None, in_=h2_dram,
                                     in_offset=bass.IndirectOffsetOnAxis(ap=gix[0:CAP, par:par + 1], axis=0),
                                     bounds_check=token_bound, oob_is_err=False).then_inc(xg_in[par], 16)

            def scatter(e, par, ahead):
                pool.wait_ge(y_evA, e + 1)
                pool.wait_ge(y_evV, e + 1)
                if not (isinstance(e, int) and e < 2):
                    pool.wait_ge(y_out[par], 8 * (e - par))
                g.tensor_copy(six[0:CAP, par:par + 1], col(pid_t, e)).then_inc(ix_ready, 1)
                pool.wait_ge(ix_ready, e + 1 + ahead)
                pool.sem_inc(pool_steps, 1)
                g.indirect_dma_start(out=y_dram, out_offset=bass.IndirectOffsetOnAxis(ap=six[0:CAP, par:par + 1], axis=0),
                                     in_=YO[par], in_offset=None, bounds_check=pair_bound,
                                     oob_is_err=False).then_inc(y_out[par], 16)

            gather(0, 0)
            gather(1, 1)

            def experts(base, last):
                for j in range(RING):
                    e = base + j
                    if not (last and j >= RING - 2):
                        gather(e + 2, j % 2)
                        scatter(e, j % 2, e + 3)
                    else:
                        scatter(e, j % 2, NE)

            experts(0, False)
            with pool.Fori(1, NE // RING - 1) as i:
                experts(i * RING, False)
            experts(NE - RING, True)
            pool.wait_ge(y_out[0], 8 * NE)
            pool.wait_ge(y_out[1], 8 * NE)
            pool.sem_inc(ov_go, 1)

            def overflow(o):
                pool.wait_ge(ov_go, o + 1)
                g.tensor_copy(gix[0:CAP, 0:1], col(tok_t, o + NE)).then_inc(ov_ix, 1)
                g.tensor_copy(six[0:CAP, 0:1], col(pid_t, o + NE)).then_inc(ov_ix, 1)
                pool.wait_ge(ov_ix, o * 2 + 2)
                pool.sem_inc(pool_steps, 1)
                g.indirect_dma_start(out=XG[0], out_offset=None, in_=h2_dram,
                                     in_offset=bass.IndirectOffsetOnAxis(ap=gix[0:CAP, 0:1], axis=0),
                                     bounds_check=token_bound, oob_is_err=False).then_inc(ov_x, 16)
                pool.wait_ge(ov_evA, o + 1)
                pool.wait_ge(ov_evV, o + 1)
                pool.sem_inc(pool_steps, 1)
                g.indirect_dma_start(out=y_dram, out_offset=bass.IndirectOffsetOnAxis(ap=six[0:CAP, 0:1], axis=0),
                                     in_=YO[0], in_offset=None, bounds_check=pair_bound,
                                     oob_is_err=False).then_inc(ov_out, 16)
                pool.wait_ge(ov_out, o * 16 + 16)
                pool.sem_inc(ov_go, 1)
            each_overflow(pool, overflow)
            pool.sem_inc(y_base, 1)
            for b in range(NB):
                pool.wait_ge(o_mul, b + 1)
                y = YG[b % 2][:, 1, :]
                g.tensor_tensor(y, y, x3[:, b, :], ALU.add).then_inc(o_add, 1)


def col(tab, e):
    return tab[0:CAP, e:e + 1] if isinstance(e, int) else tab[0:CAP, bass.ds(e, 1)]


INPUTS = ["x", "c", "positions", "g_pre_mix", "w_ada", "b_ada", "w_in", "w_out", "g_post_mix", "g_pre_ffn", "w_group",
          "b_group", "w_expert", "b_expert", "w_gate_exp", "w_up_exp", "w_down_exp", "g_post_ffn"]


def kernel(**inputs):
    import concourse.bacc as bacc
    from concourse.bass_utils import run_bass_kernel_spmd

    nc = bacc.Bacc("TRN2", target_bir_lowering=False, num_devices=1)
    cst, decay, pair = shape_constants()
    given = {name: np.ascontiguousarray(inputs[name]) for name in INPUTS}
    given.update(cst=cst, decay=decay, pair=pair)
    arrays, tensors = {}, {}
    for name, a in given.items():
        arrays[f"in_{name}"] = a
        tensors[name] = nc.dram_tensor(f"in_{name}", a.shape, mybir.dt.from_np(a.dtype), kind="ExternalInput").ap()
    out = nc.dram_tensor("out", (1, S, D), F32, kind="ExternalOutput").ap()
    build(nc, tensors, out)
    r = run_bass_kernel_spmd(nc, [arrays], core_ids=[0])
    return r.results[0]["out"]
```

```python
from contextlib import ExitStack
import math

import numpy as np
import concourse.bass as bass
from concourse import mybir

P = 128
D = 1024
S = 512
NB = S // P
KD = D // P
HEADS, DH = 8, 64
RHEADS, RDH = 4, 128
TOPK = min(256, S // 4)
NG, EPG = 4, 8
NE = NG * EPG
F = 256
KF = F // P
EPS = 1e-6
NEG = -1.0e30
TAKEN = -3.0e38
IDX_SCALE = (HEADS ** -0.5) * (DH ** -0.5)
ATT_SCALE = DH ** -0.5
MAGIC = 1.5 * 2.0 ** 23

TWO_PI = (6.28125, 0.0019350051879882812, 3.019916050268e-07)
CAP = 96
NOV = 2 * S // CAP
NT = NE + NOV
NM = (S + CAP - 1) // CAP
NOBODY = 8 * S
RING = 4
CHUNK = KD * 512
SLOT = KD * F * 2 + KF * D

ALU = mybir.AluOpType
ACT = mybir.ActivationFunctionType
AX = mybir.AxisListType.X
F32 = mybir.dt.float32
I32 = mybir.dt.int32
U32 = mybir.dt.uint32

COL = {"qa": 0, "ka": 512, "va": 1024, "qi": 1536, "kw": 2048, "qr": 2120, "kr": 2632, "vr": 3144, "gr": 3656}
KW = DH + HEADS
ROPE = {"kw": DH, "qi": DH, "qa": DH, "ka": DH, "qr": RDH, "kr": RDH}
ITEMS = ([("ada", 0), ("ada", 1), ("ada", 2), ("ada", 3), ("in", "kw"), ("in", "qi"), ("ada", 4), ("in", "qr"),
          ("ada", 5), ("in", "kr"), ("ada", 6), ("in", "vr"), ("ada", 7), ("in", "gr"), ("ada", 8), ("in", "ka"),
          ("ada", 9), ("in", "qa"), ("ada", 10), ("in", "va"), ("ada", 11), ("out", 0), ("out", 1), ("router", 0)])
AT = {item: n for n, item in enumerate(ITEMS)}
assert len(ITEMS) % RING == 0 and NE % RING == 0
EARLY = len(ITEMS) // RING

C_ID, C_CAUSAL, C_LT, C_ONES, C_FREQ, C_IOTA = 0, 128, 256, 384, 512, 576
C_PAIR = C_IOTA + P
C_EPS = C_PAIR + 2 * NB
C_ZERO = C_EPS + 1
NCONST = C_ZERO + 1


def shape_constants():
    c = np.zeros((P, NCONST), np.float32)
    i = np.arange(P)
    c[:, C_ID:C_ID + P] = np.eye(P)
    c[:, C_CAUSAL:C_CAUSAL + P] = np.where(i[None, :] <= i[:, None], 0.0, NEG)
    c[:, C_LT:C_LT + P] = i[:, None] < i[None, :]
    c[:, C_ONES:C_ONES + P] = 1.0
    c[:, C_FREQ:C_FREQ + 64] = np.float32(10000.0) ** (-np.arange(64, dtype=np.float32) / np.float32(64))
    c[:, C_IOTA:C_IOTA + P] = i
    c[:, C_EPS] = EPS
    g = 1.0 - 2.0 ** (-5.0 - np.arange(RHEADS))
    diff = np.arange(S)[None, None, :] - i[:, None, None]
    decay = np.where(diff >= 0, np.exp(np.log(g)[None, :, None] * np.maximum(diff, 0)), 0.0) * RDH ** -0.5
    pair = (np.arange(NB)[None, :, None] * P + i[:, None, None]) * 2 + np.arange(2)[None, None, :]
    c[:, C_PAIR:C_PAIR + 2 * NB] = pair.reshape(P, 2 * NB) + 1
    return c, decay.reshape(P, RHEADS * S).astype(np.float32)


ORDER = ["kw", "qi", "qr", "IDX", ("MOD", 2), "kr", "vr", ("MOD", 3), "gr", "ka", ("MOD", 4), "RET", "qa", "va",
         "RETT", "ATT", ("MOD", 5), "OUT"]
AHEADS = [(b, h) for b in range(NB) for h in range(HEADS)]


class Plan:

    def __init__(self):
        self.bank, self.before, last = {}, {}, {}
        self.tp, self.sc, self.rope, self.unit, self.o = {}, {}, {}, {}, 0
        self.v = {}

        def use(name, bank, width=1):
            self.bank[name] = bank
            self.before[name] = [last[b] for b in range(bank, bank + width) if b in last]
            for b in range(bank, bank + width):
                last[b] = name

        def turn(name):
            self.tp[name] = len(self.tp)
            use(name, 2 + self.tp[name] % 2)

        def score(name):
            self.sc[name] = len(self.sc)
            use(name, 4 + self.sc[name] % 2)

        def output(name):
            use(name, 6 + self.o % 2)
            self.o += 1

        self.steps = []
        waiting = None
        output(("modA",))
        for k in range(KD):
            self.tp[("x", k)] = k
            use(("x", k), (0, 1, 2, 3, 4, 5, 7, 0)[k])
        for s in ORDER:
            if s in COL:
                for b in range(NB):
                    name = ("unit", s, b)
                    self.unit[name] = len(self.unit)
                    use(name, self.unit[name] % 2)
                    self.steps.append(name)
                    if waiting:
                        turn(waiting)
                        self.steps.append(waiting)
                        waiting = None
                    if s in ROPE:
                        self.rope[name] = len(self.rope)
                        waiting = ("turn", s, b)
                    if s in ("vr", "va"):
                        self.v[name] = len(self.v)
                continue
            s = s if isinstance(s, tuple) else (s,)
            self.steps.append(s)
            if s[0] == "MOD":
                output(s + (0,))
                output(s + (1,))
            elif s[0] == "IDX":
                for b in range(1, NB):
                    for h in range(HEADS):
                        score(("idx", b, h))
            elif s[0] == "RET":
                for h in range(RHEADS):
                    for j in range(NB):
                        score(("ret", h, j))
                    output(("reto", h))
            elif s[0] == "RETT":
                for b in range(NB):
                    turn(("rett", b))
            elif s[0] == "ATT":
                for u in range(len(AHEADS) + 4):
                    if u < len(AHEADS):
                        score(("att",) + AHEADS[u])
                    if 2 <= u < len(AHEADS) + 2:
                        turn(("pt",) + AHEADS[u - 2])
                    if 3 <= u < len(AHEADS) + 3 and AHEADS[u - 3][1] == 0:
                        output(("atto", AHEADS[u - 3][0]))
                    if u >= 4 and AHEADS[u - 4][1] == HEADS - 1:
                        turn(("attt", AHEADS[u - 4][0]))
            elif s[0] == "OUT":
                for b in range(NB):
                    use(("wout", b), (0, 6)[b % 2], 2)
                for b in range(NB):
                    turn(("h2", b, 0))
                    turn(("h2", b, 1))
                use(("router",), 4)
                use(("rank",), 5)
                use(("table",), 4)


def build(nc, t, out):
    plan = Plan()
    steps = plan.steps

    with ExitStack() as ctx:
        def sb(name, words, dt=F32, parts=P):
            return ctx.enter_context(nc.sbuf_tensor(name, [parts, words], dt))

        def sem(name):
            return ctx.enter_context(nc.semaphore(name))

        psum = ctx.enter_context(nc.psum_tensor("psum", [P, 8 * 512], F32))
        ps = [psum[:, i * 512:(i + 1) * 512] for i in range(8)]

        ring = sb("ring", RING * SLOT)
        xs = sb("xs", NB * D)
        hT = sb("hT", KD * S)
        work = sb("work", 4 * 2048 + 512)
        retbuf = sb("retbuf", 2560)
        ropebuf = sb("ropebuf", 2048)
        accB = sb("accB", D)
        G1 = sb("G1", D)
        S2 = sb("S2", D)
        T2 = sb("T2", D)
        score = sb("score", P * (2 + 3 + 4))
        cst = sb("cst", NCONST)
        cosT = sb("cosT", NB * 64)
        sinT = sb("sinT", NB * 64)
        sm = sb("sm", 256)
        rb = sb("rb", 36)
        posi = sb("posi", NB, I32)
        pid_t = sb("pid_t", NT, U32)
        tok_t = sb("tok_t", NT, U32)
        ctl = sb("ctl", NOV + 1, I32)
        gix = sb("gix", RING, U32)
        six = sb("six", 2, U32)

        x3 = xs[:, :].rearrange("p (b d) -> p b d", b=NB)
        hT3 = hT[:, :].rearrange("p (k t) -> p k t", k=KD)
        ident = cst[:, C_ID:C_ID + P]
        ones = cst[:, C_ONES:C_ONES + P]

        qaT = work[:, 0:2048].rearrange("p (c t) -> p c t", c=4)
        kaT = work[:, 2048:4096].rearrange("p (c t) -> p c t", c=4)
        va = work[:, 4096:6144].rearrange("p (b e) -> p b e", b=NB)
        qiT = work[:, 6144:8192].rearrange("p (c t) -> p c t", c=4)
        kiT = work[:, 8192:8704]
        decay = work[:, 0:2048].rearrange("p (h t) -> p h t", h=RHEADS)
        xn = work[:, 0:4096].rearrange("p (b d) -> p b d", b=NB)
        accA = work[:, 4096:6144].rearrange("p (m n) -> p m n", m=2)
        Rsb = work[:, 6144:8192].rearrange("p (b e) -> p b e", b=NB)

        def tail(s):
            return ring[:, s * SLOT + CHUNK:(s + 1) * SLOT]
        qrT = tail(0).rearrange("p (c t) -> p c t", c=4)
        krT = tail(1).rearrange("p (c t) -> p c t", c=4)
        vr = tail(2).rearrange("p (b e) -> p b e", b=NB)
        gr = tail(3).rearrange("p (b e) -> p b e", b=NB)

        def chunk(n, cols=512):
            s = n % RING
            return ring[:, s * SLOT:s * SLOT + KD * cols].rearrange("p (k n) -> p k n", k=KD)

        def expert(s):
            base = s * SLOT
            w = KD * F
            return (ring[:, base:base + w].rearrange("p (k n) -> p k n", k=KD),
                    ring[:, base + w:base + 2 * w].rearrange("p (k n) -> p k n", k=KD),
                    ring[:, base + 2 * w:base + SLOT].rearrange("p (i n) -> p i n", i=KF))

        def cols(at, n):
            return sm[:, at:at + n]
        cc, sc_, cg, cb = cols(0, 8), cols(8, 8), cols(16, 8), cols(24, 16)
        gs1, sh1 = cols(40, 8), cols(48, 8)
        ss1, r1 = cols(56, 4), cols(60, 4)
        posf = cols(64, 4)
        wi = cols(68, 32).rearrange("p (b h) -> p b h", b=NB)
        ssr, rr = cols(100, 16), cols(116, 16)
        nmx, rsum, rinv = cols(132, 2), cols(134, 32).rearrange("p (b h) -> p b h", b=NB), cols(166, 8)
        ssm, rm = cols(174, 4), cols(186, 4)
        ss2, r2 = cols(190, 4), cols(194, 4)
        wts = cols(198, 8).rearrange("p (b j) -> p b j", b=NB)
        ctmp = cols(206, 16)
        modA_s = cols(222, 16)
        yss, yr = cols(238, 4), cols(242, 4)
        top8 = cols(248, 8)

        x_in, decay_in = sem("x_in"), sem("decay_in")
        cst_in, c_in, pre_in, post_in = sem("cst_in"), sem("c_in"), sem("pre_in"), sem("post_in")
        landed = [sem(f"landed{s}") for s in range(RING)]
        ada_done = sem("ada_done")
        v_chain = sem("v_chain")
        c_exp, c_silu = sem("c_exp"), sem("c_silu")
        x_ss, x_sq, x_r, x_n = sem("x_ss"), sem("x_sq"), sem("x_r"), sem("x_n")
        wout_done = sem("wout_done")
        ang_ready, trig_ready = sem("ang_ready"), sem("trig_ready")
        modA_done, gs_ready = sem("modA_done"), sem("gs_ready")
        unit_done, tp_done, sc_done, o_done = sem("unit_done"), sem("tp_done"), sem("sc_done"), sem("o_done")
        rope_ab, roped = sem("rope_ab"), sem("roped")
        evac = sem("evac")
        v_ready = sem("v_ready")
        g_exp, g_ready = sem("g_exp"), sem("g_ready")
        relu_ready, relu_used = sem("relu_ready"), sem("relu_used")
        mod_done, mod_ready = sem("mod_done"), sem("mod_ready")
        it_ready, it_used = sem("it_ready"), sem("it_used")
        R_ready, ret_ss, ret_sq, ret_ready = sem("R_ready"), sem("ret_ss"), sem("ret_sq"), sem("ret_ready")
        att_max, att_exp = sem("att_max"), sem("att_exp")
        att_ready = sem("att_ready")
        mix_ss, mix_sq, mix_n = sem("mix_ss"), sem("mix_sq"), sem("mix_n")
        res_ready, res_ss, res_sq = sem("res_ready"), sem("res_ss"), sem("res_sq")
        h2_ready = sem("h2_ready")
        h2_out = [sem("h2_out0"), sem("h2_out1")]
        g_sub, g_exped, d_sub, d_exped = sem("g_sub"), sem("g_exped"), sem("d_sub"), sem("d_exped")
        oh_ready, rank_done, slot_ready, table_done, tok_ready = (
            sem("oh_ready"), sem("rank_done"), sem("slot_ready"), sem("table_done"), sem("tok_ready"))
        router_done = sem("router_done")
        xg_in = [sem(f"xg_in{i}") for i in range(RING)]
        xg_clear, xt_mm, xt_ev = sem("xg_clear"), sem("xt_mm"), sem("xt_ev")
        gu_mm, gu_exp, gu_step, hid_ready = sem("gu_mm"), sem("gu_exp"), sem("gu_step"), sem("hid_ready")
        y_mm, y_evA, y_evV = sem("y_mm"), sem("y_evA"), sem("y_evV")
        y_out = [sem("y_out0"), sem("y_out1")]
        yw_ready, y_ss, y_sq, o_add = sem("yw_ready"), sem("y_ss"), sem("y_sq"), sem("o_add")
        y_back = [sem(f"y_back{b}") for b in range(NB)]
        o_out = sem("o_out")
        lg_ready, ix_ready = sem("lg_ready"), sem("ix_ready")
        pool_steps = sem("pool_steps")
        ctl_ready, ov_go, ov_w, ov_x, ov_turned, ov_brought = (sem("ctl_ready"), sem("ov_go"), sem("ov_w"),
                                                               sem("ov_x"), sem("ov_turned"), sem("ov_brought"))
        ov_gu, ov_exp, ov_step, ov_hid, ov_y, ov_evA, ov_evV, ov_ix, ov_out = (
            sem("ov_gu"), sem("ov_exp"), sem("ov_step"), sem("ov_hid"), sem("ov_y"), sem("ov_evA"), sem("ov_evV"),
            sem("ov_ix"), sem("ov_out"))
        g2_in, accB_clear, bias_in = sem("g2_in"), sem("accB_clear"), sem("bias_in")
        y_base = sem("y_base")

        h2_dram = nc.dram_tensor("h2_rows", [S, D], F32, kind="Internal").ap()
        y_dram = nc.dram_tensor("pair_rows", [2 * S, D], F32, kind="Internal").ap()

        w_ada = t["w_ada"].rearrange("l (p k) n -> (l p) k n", k=KD)
        w_in = t["w_in"].rearrange("l (p k) n -> (l p) k n", k=KD)
        w_out = t["w_out"].rearrange("l (k p) n -> (l p) k n", k=KD)
        w_grp = t["w_group"].rearrange("l (p k) n -> (l p) k n", k=KD)
        w_exp = t["w_expert"].rearrange("l (p k) n -> (l p) k n", k=KD)
        wg_d = t["w_gate_exp"].rearrange("l e (p k) n -> (l e) p (k n)", k=KD)
        wu_d = t["w_up_exp"].rearrange("l e (p k) n -> (l e) p (k n)", k=KD)
        wd_d = t["w_down_exp"].rearrange("l e (p i) n -> (l e) p (i n)", i=KF)
        b_ada = t["b_ada"].rearrange("l (m n) -> (l m) n", n=D)

        def pcol(name):
            return t[name].rearrange("l (p k) -> (l p) k", k=KD)

        def prow(ap, n):
            return ap.broadcast_to([P, n])

        block = ctx.enter_context(nc.Block())

        def bank(use):
            return ps[plan.bank[use]]

        def read_out(use):
            kind = use[0]
            if use in plan.tp:
                return evac, plan.tp[use] + 1
            if use in plan.rope:
                return rope_ab, plan.rope[use] + 1
            if use in plan.v:
                return v_ready, plan.v[use] + 1
            if kind == "unit":
                return g_ready, use[2] + 1
            return {"modA": lambda: (gs_ready, 2),
                    "router": lambda: (lg_ready, 1),
                    "MOD": lambda: (mod_ready, 2 * (use[1] - 2) + use[2] + 1),
                    "idx": lambda: (relu_ready, plan.sc[use] + 1),
                    "ret": lambda: (it_ready, NB * use[1] + use[2] + 1),
                    "reto": lambda: (R_ready, use[1] + 1),
                    "att": lambda: (att_max, use[1] * HEADS + use[2] + 1),
                    "atto": lambda: (att_ready, use[1] + 1),
                    "wout": lambda: (mix_n, use[1] + 1)}[kind]()

        def take(pe, use):
            for earlier in plan.before[use]:
                pe.wait_ge(*read_out(earlier))
            return ps[plan.bank[use]]

        def used_up(item):
            kind, what = item
            if kind == "ada":
                return ada_done, what + 1
            if kind == "in":
                return unit_done, plan.unit[("unit", what, NB - 1)] + 1
            return (wout_done, NB) if kind == "out" else (router_done, NB)

        def brought(use):
            return evac, plan.tp[use] + 1

        XG = [work[0:CAP, (4 + i) * D:(5 + i) * D] for i in range(RING)]
        XT = [hT[:, i * KD * CAP:(i + 1) * KD * CAP].rearrange("p (k c) -> p k c", k=KD)
              for i in range(2)]
        YO = [work[0:CAP, i * D:(i + 1) * D] for i in range(2)]
        W2 = KF * CAP
        EG = [work[:, 2048 + i * W2:2048 + (i + 1) * W2] for i in range(2)]
        HID = [work[:, 2048 + (2 + i) * W2:2048 + (3 + i) * W2].rearrange("p (i c) -> p i c", i=KF) for i in range(2)]
        GUM = work[:, 2048 + 4 * W2:2048 + 5 * W2]
        YG = [at.rearrange("p (j d) -> p j d", j=2) for at in (work[:, 4 * D:6 * D], work[:, 6 * D:8 * D],
                                                               hT[:, 0:2 * D], hT[:, 2 * D:4 * D])]

        def load_expert(sp, e, s, signal=None):
            signal = signal or landed[s]
            w = KD * F
            base = s * SLOT
            sp.dma_start(ring[:, base:base + w], pick(wg_d, e)).then_inc(signal, 16)
            sp.dma_start(ring[:, base + w:base + 2 * w], pick(wu_d, e)).then_inc(signal, 16)
            sp.dma_start(ring[:, base + 2 * w:base + SLOT], pick(wd_d, e)).then_inc(signal, 16)

        def pick(ap, e):
            return ap[e, :, :] if isinstance(e, int) else ap[bass.ds(e, 1), :, :].rearrange("a p n -> (a p) n")

        def land(eng, n):
            extra = 16 if n == AT[("router", 0)] else 0
            eng.wait_ge(landed[n % RING], 16 * (n // RING + 1) + extra)

        def landed_by(e, s):
            early = 16 * EARLY + (16 if s == AT[("router", 0)] % RING else 0)
            return early + 12 * (e - s) + 48

        def iT(h, j):
            at = (0, 512, 896, 1152)[j] + (h % 2) * 1280
            return retbuf[:, at:at + S - j * P]

        zero = cst[:, C_ZERO:C_ZERO + 1]
        eps = cst[:, C_EPS:C_EPS + 1]

        def each_overflow(eng, work_on):
            eng.wait_ge(ctl_ready, 1)
            count = eng.value_load(ctl[0:1, NOV:NOV + 1], min_val=0, max_val=NOV)
            with eng.If(count > 0):
                with eng.Fori(0, count) as o:
                    work_on(o)

        RELU = [retbuf[:, i * 512:(i + 1) * 512] for i in range(2)]
        SMX = [ropebuf[:, i * 512:(i + 1) * 512] for i in range(2)]
        PEX = [ropebuf[:, 1024 + i * 512:1536 + i * 512] for i in range(2)]
        ATO = [retbuf[:, i * 512:(i + 1) * 512] for i in range(2)]
        PTS = [retbuf[:, 1024 + i * 512:1536 + i * 512] for i in range(2)]
        MIXN = [work[:, i * D:(i + 1) * D] for i in range(2)]
        H2 = [work[:, i * D:(i + 1) * D] for i in (2, 7)]
        G2 = work[:, 3 * D:4 * D]
        H2T = [work[:, (4 + i) * D:(5 + i) * D].rearrange("p (k t) -> p k t", k=KD) for i in range(2)]
        JUNK = work[:, 6 * D:7 * D]
        JUNK2 = work[:, 0:D]
        out_blocks = out.rearrange("a (b p) d -> (a b) p d", p=P)
        def rt(at, n):
            return retbuf[:, at:at + NB * n].rearrange("p (b n) -> p b n", b=NB)
        LG, GMAX, GSUBV, GEXV, GSUM, GTOP = rt(0, 36), rt(144, 1), rt(152, NG), rt(168, NG), rt(184, 1), rt(188, 1)
        GT, GM, SG = rt(192, NG), rt(208, 1), rt(212, NG)
        OH = rt(256, NE)
        EL, EMAX, ET, EM, O1, EL2, EMAX2, O2 = (rt(512, EPG), rt(544, 1), rt(548, EPG), rt(580, 1), rt(584, EPG),
                                                rt(616, EPG), rt(648, 1), rt(652, EPG))
        DSUB, P2, WT = rt(684, 1), rt(688, 1), rt(692, 1)
        OH1, OH2, RANK = rt(704, NE), rt(832, NE), rt(960, NE)
        CNT, OV, BINC, BEX = (retbuf[:, 1088:1120], retbuf[:, 1248:1280], retbuf[:, 1280:1312], retbuf[:, 1312:1344])
        MFL, QT, TMP = rt(1120, NE), rt(1344, NE), rt(1600, NE)
        TILE, ROW = (retbuf[:, at:at + 2 * NB].rearrange("p (b j) -> p b j", b=NB) for at in (1728, 1736))
        OVC = retbuf[:, 1760:1760 + NOV * NE].rearrange("p (o e) -> p o e", o=NOV)
        EO = retbuf[:, 2400:2400 + NOV]
        IN_ROW = ropebuf[:, 0:2 * NB * CAP].rearrange("p (n c) -> p n c", n=2 * NB)
        IN_TILE = ropebuf[:, 1024:1024 + 2 * NB * NT].rearrange("p (n t) -> p n t", n=2 * NB)
        EMPTY, IDS = (ropebuf[0:CAP, 1536 + i * NT:1536 + (i + 1) * NT] for i in range(2))

        @block.sync
        def _(sp):
            sp.dma_start(cst[:, :], t["cst"]).then_inc(cst_in, 16)
            for n, (kind, what) in enumerate(ITEMS):
                s = n % RING
                if n >= RING:
                    sp.wait_ge(*used_up(ITEMS[n - RING]))
                if kind == "ada":
                    sp.dma_start(chunk(n), w_ada[:, :, what * 512:(what + 1) * 512]).then_inc(landed[s], 16)
                elif kind == "in":
                    width = KW if what == "kw" else 512
                    sp.dma_start(chunk(n, width), w_in[:, :, COL[what]:COL[what] + width]).then_inc(landed[s], 16)
                elif kind == "out":
                    sp.dma_start(chunk(n), w_out[:, :, what * 512:(what + 1) * 512]).then_inc(landed[s], 16)
                else:
                    r = chunk(n, NG + NE)
                    sp.dma_start(r[:, :, 0:NG], w_grp).then_inc(landed[s], 16)
                    sp.dma_start(r[:, :, NG:NG + NE], w_exp).then_inc(landed[s], 16)
                if (kind, what) == ("ada", 1):
                    sp.dma_start(x3, t["x"].rearrange("a (b p) d -> (a p) b d", p=P)).then_inc(x_in, 16)
                if (kind, what) == ("in", "kw"):
                    sp.wait_ge(tp_done, KD)
                    sp.dma_start(work[:, 0:RHEADS * S], t["decay"]).then_inc(decay_in, 16)
            sp.wait_ge(ret_ready, NB)
            for e in range(RING):
                sp.wait_ge(*used_up(ITEMS[len(ITEMS) - RING + e]))
                load_expert(sp, e, e)
            with sp.Fori(1, NE // RING) as i:
                for j in range(RING):
                    sp.wait_ge(y_mm, i * 2 * RING + (2 * j + 2 - 2 * RING))
                    load_expert(sp, i * RING + j, j)
            sp.wait_ge(y_mm, 2 * NE)

            def overflow(o):
                sp.wait_ge(ov_go, o + 1)
                load_expert(sp, sp.value_load(ctl[0:1, bass.ds(o, 1)], min_val=0, max_val=NE - 1), 0, ov_w)
            each_overflow(sp, overflow)
            for b in range(NB):
                sp.wait_ge(o_add, b + 1)
                sp.dma_start(out_blocks[b], YG[b][:, 1, :]).then_inc(o_out, 16)
            sp.wait_ge(o_out, 16 * NB)

        @block.tensor
        def _(pe):
            def chunk_unit(name, b):
                n = AT[("in", name)]
                width = KW if name == "kw" else 512
                w = chunk(n, width)
                if b == 0:
                    land(pe, n)
                    if name == "kw":
                        pe.wait_ge(*brought(("x", KD - 1)))
                o = take(pe, ("unit", name, b))
                for k in range(KD):
                    mm = pe.matmul(o[:, 0:width], hT3[:, k, b * P:(b + 1) * P], w[:, k, :], start=(k == 0),
                                   stop=(k == KD - 1))
                mm.then_inc(unit_done, 1)

            def turn(name, b):
                use = ("turn", name, b)
                r = plan.rope[("unit", name, b)]
                o = take(pe, use)
                pe.wait_ge(roped, r + 1)
                src = ropebuf[:, 1024 + (r % 2) * 512:1536 + (r % 2) * 512]
                for c in range(1 if name == "kw" else 4):
                    mm = pe.transpose(o[:, c * P:(c + 1) * P], src[:, c * P:(c + 1) * P], ident)
                mm.then_inc(tp_done, 1)

            def sum_mod(m):
                pe.wait_ge(ada_done, 2 * m + 2)
                o = bank(("modA",))
                a = accA[:, m, :].rearrange("p (q k) -> p k q", k=KD)
                for k in range(KD):
                    mm = pe.matmul(o[:, m * KD + k:m * KD + k + 1], a[:, k, :], ones[:, 0:1], start=True, stop=True)
                mm.then_inc(modA_done, 1)

            pe.wait_ge(cst_in, 16)
            sum_mod(0)
            pe.wait_ge(x_n, NB)
            for k in range(KD):
                if k == KD - 1:
                    sum_mod(1)
                o = take(pe, ("x", k))
                for b in range(NB):
                    v = xn[:, b, :].rearrange("p (q k) -> p k q", k=KD)
                    mm = pe.transpose(o[:, b * P:(b + 1) * P], v[:, k, :], ident)
                mm.then_inc(tp_done, 1)

            def mod(m):
                pe.wait_ge(ada_done, 2 * m + 2)
                for n in range(2):
                    o = take(pe, ("MOD", m, n))
                    pe.matmul(o[:, :], ones, accB[:, n * 512:(n + 1) * 512], start=True, stop=True).then_inc(mod_done, 1)

            def idx():
                pe.wait_ge(*brought(("turn", "qi", NB - 1)))
                for b in range(1, NB):
                    for h in range(HEADS):
                        n = (b + 1) * P
                        lo = DH * (h % 2)
                        o = take(pe, ("idx", b, h))
                        pe.matmul(o[:, 0:n], qiT[lo:lo + DH, h // 2, b * P:(b + 1) * P], kiT[lo:lo + DH, 0:n],
                                  start=True, stop=True).then_inc(sc_done, 1)

            def retention():
                pe.wait_ge(*brought(("turn", "kr", NB - 1)))
                pe.wait_ge(v_ready, NB)
                for h in range(RHEADS + 1):
                    if h < RHEADS:
                        for j in range(NB):
                            n = S - j * P
                            o = take(pe, ("ret", h, j))
                            pe.matmul(o[:, 0:n], krT[:, h, j * P:(j + 1) * P], qrT[:, h, j * P:S], start=True,
                                      stop=True).then_inc(sc_done, 1)
                    if h >= 1:
                        g = h - 1
                        o = take(pe, ("reto", g))
                        pe.wait_ge(it_ready, NB * (g + 1))
                        for i in range(NB):
                            for j in range(i + 1):
                                mm = pe.matmul(o[:, i * P:(i + 1) * P], iT(g, j)[:, (i - j) * P:(i - j + 1) * P],
                                               vr[:, j, g * RDH:(g + 1) * RDH], start=(j == 0), stop=(j == i))
                        mm.then_inc(o_done, 1)

            def retention_turn():
                for b in range(NB):
                    o = take(pe, ("rett", b))
                    pe.wait_ge(ret_ready, b + 1)
                    for c in range(4):
                        mm = pe.transpose(o[:, c * P:(c + 1) * P], Rsb[:, b, c * P:(c + 1) * P], ident)
                    mm.then_inc(tp_done, 1)

            def attention():
                def scores(b, h):
                    n = (b + 1) * P
                    lo = DH * (h % 2)
                    o = take(pe, ("att", b, h))
                    pe.matmul(o[:, 0:n], qaT[lo:lo + DH, h // 2, b * P:(b + 1) * P], kaT[lo:lo + DH, h // 2, 0:n],
                              start=True, stop=True).then_inc(sc_done, 1)

                def turn_p(b, h):
                    u = b * HEADS + h
                    o = take(pe, ("pt", b, h))
                    pe.wait_ge(att_exp, u + 1)
                    for j in range(b + 1):
                        mm = pe.transpose(o[:, j * P:(j + 1) * P], PEX[u % 2][:, j * P:(j + 1) * P], ident)
                    mm.then_inc(tp_done, 1)

                def values(b, h):
                    u = b * HEADS + h
                    if h == 0:
                        take(pe, ("atto", b))
                    o = bank(("atto", b))
                    pe.wait_ge(*brought(("pt", b, h)))
                    for j in range(b + 1):
                        mm = pe.matmul(o[:, h * DH:(h + 1) * DH], PTS[u % 2][:, j * P:(j + 1) * P],
                                       va[:, j, h * DH:(h + 1) * DH], start=(j == 0), stop=(j == b))
                    mm.then_inc(o_done, 1)

                def turn_o(b):
                    o = take(pe, ("attt", b))
                    pe.wait_ge(att_ready, b + 1)
                    for c in range(4):
                        mm = pe.transpose(o[:, c * P:(c + 1) * P], ATO[b % 2][:, c * P:(c + 1) * P], ident)
                    mm.then_inc(tp_done, 1)

                pe.wait_ge(*brought(("turn", "qa", NB - 1)))
                pe.wait_ge(v_ready, 2 * NB)
                heads = [(b, h) for b in range(NB) for h in range(HEADS)]
                for u in range(len(heads) + 4):
                    if u < len(heads):
                        scores(*heads[u])
                    if 2 <= u < len(heads) + 2:
                        turn_p(*heads[u - 2])
                    if 3 <= u < len(heads) + 3:
                        values(*heads[u - 3])
                    if u >= 4 and heads[u - 4][1] == HEADS - 1:
                        turn_o(heads[u - 4][0])

            def project():
                def wout(b):
                    if b == 0:
                        pe.wait_ge(*brought(("attt", NB - 1)))
                        land(pe, AT[("out", 0)])
                        land(pe, AT[("out", 1)])
                    take(pe, ("wout", b))
                    for n in range(2):
                        o = ps[plan.bank[("wout", b)] + n]
                        w = chunk(AT[("out", n)])
                        for k in range(KD):
                            mm = pe.matmul(o[:, :], hT3[:, k, b * P:(b + 1) * P], w[:, k, :], start=(k == 0),
                                           stop=(k == KD - 1))
                    mm.then_inc(wout_done, 1)

                def turn_h2(b):
                    pe.wait_ge(h2_ready, b + 1)
                    for q in range(2):
                        o = take(pe, ("h2", b, q))
                        v = H2[b % 2].rearrange("p (q k) -> p k q", k=KD)
                        for c in range(4):
                            mm = pe.transpose(o[:, c * P:(c + 1) * P], v[:, 4 * q + c, :], ident)
                        mm.then_inc(tp_done, 1)

                def route(b):
                    pe.wait_ge(*brought(("h2", b, 1)))
                    if b == 0:
                        land(pe, AT[("router", 0)])
                        take(pe, ("router",))
                    w = chunk(AT[("router", 0)], NG + NE)
                    o = bank(("router",))
                    for k in range(KD):
                        mm = pe.matmul(o[:, b * 36:b * 36 + 36], H2T[b % 2][:, k, :], w[:, k, :], start=(k == 0),
                                       stop=(k == KD - 1))
                    mm.then_inc(router_done, 1)

                for b in range(NB + 2):
                    if b < NB:
                        wout(b)
                    if 1 <= b <= NB:
                        turn_h2(b - 1)
                    if b >= 2:
                        route(b - 2)
                pe.wait_ge(oh_ready, 1)
                o = take(pe, ("rank",))
                for b in range(NB):
                    for q in range(b + 1):
                        pe.matmul(o[:, b * NE:(b + 1) * NE], cst[:, C_LT:C_LT + P] if q == b else ones,
                                  OH[:, q, :], start=(q == 0), stop=(q == b))
                for q in range(NB):
                    mm = pe.matmul(o[:, NB * NE:(NB + 1) * NE], ones, OH[:, q, :], start=(q == 0), stop=(q == NB - 1))
                mm.then_inc(rank_done, 1)
                pe.wait_ge(slot_ready, 1)
                o = take(pe, ("table",))
                for n in range(2 * NB):
                    mm = pe.matmul(o[0:CAP, 0:NT], IN_ROW[:, n, :], IN_TILE[:, n, :], start=(n == 0),
                                   stop=(n == 2 * NB - 1))
                mm.then_inc(table_done, 1)

            for s in steps:
                if s[0] == "unit":
                    chunk_unit(*s[1:])
                elif s[0] == "turn":
                    turn(*s[1:])
                elif s[0] == "MOD":
                    mod(s[1])
                elif s[0] == "IDX":
                    idx()
                elif s[0] == "RET":
                    retention()
                elif s[0] == "RETT":
                    retention_turn()
                elif s[0] == "ATT":
                    attention()
                else:
                    project()

            def turn_x(e, s):
                pe.wait_ge(xg_in[s], 4 * (e - s) + 16)
                for q in range(2):
                    if not (isinstance(e, int) and e == 0):
                        pe.wait_ge(xt_ev, 2 * e - 1 + q)
                    v = XG[s].rearrange("p (q k) -> p k q", k=KD)
                    for c in range(4):
                        mm = pe.transpose(ps[2 + q][:, c * CAP:(c + 1) * CAP], v[:, 4 * q + c, :],
                                          cst[0:CAP, C_ID:C_ID + CAP])
                    mm.then_inc(xt_mm, 1)

            def gate_up(e, s):
                par = s % 2
                pe.wait_ge(landed[s], landed_by(e, s))
                pe.wait_ge(xt_ev, 2 * e + 2)
                if not (isinstance(e, int) and e < 2):
                    pe.wait_ge(hid_ready, e - 1)
                wg, wu, _ = expert(s)
                o = ps[4 + par]
                for m, w in enumerate((wg, wu)):
                    for i in range(KF):
                        c = (m * KF + i) * CAP
                        wv = w.rearrange("p k (q i) -> p k i q", i=KF)
                        for k in range(KD):
                            mm = pe.matmul(o[:, c:c + CAP], wv[:, k, i, :], XT[par][:, k, :], start=(k == 0),
                                           stop=(k == KD - 1))
                mm.then_inc(gu_mm, 1)

            def down(e, s):
                par = s % 2
                pe.wait_ge(hid_ready, e + 1)
                if not (isinstance(e, int) and e < 2):
                    pe.wait_ge(y_evA, e - 1)
                    pe.wait_ge(y_evV, e - 1)
                wd = expert(s)[2]
                for n in range(2):
                    o = ps[(0, 6)[par] + n]
                    for i in range(KF):
                        mm = pe.matmul(o[0:CAP, :], HID[par][:, i, :], wd[:, i, n * 512:(n + 1) * 512],
                                       start=(i == 0), stop=(i == KF - 1))
                    mm.then_inc(y_mm, 1)

            turn_x(0, 0)
            turn_x(1, 1)
            gate_up(0, 0)

            def experts(base, last):
                for j in range(RING):
                    e = base + j
                    if not (last and j == RING - 1):
                        gate_up(e + 1, (j + 1) % RING)
                    if not (last and j >= RING - 2):
                        turn_x(e + 2, (j + 2) % RING)
                    down(e, j)

            experts(0, False)
            with pe.Fori(1, NE // RING - 1) as i:
                experts(i * RING, False)
            experts(NE - RING, True)

            def overflow(o):
                pe.wait_ge(ov_x, o * 16 + 16)
                rows = XG[0].rearrange("p (q k) -> p k q", k=KD)
                for k in range(KD):
                    mm = pe.transpose(ps[2 + k // 4][:, (k % 4) * CAP:(k % 4 + 1) * CAP], rows[:, k, :],
                                      cst[0:CAP, C_ID:C_ID + CAP])
                mm.then_inc(ov_turned, 1)
                pe.wait_ge(ov_brought, o + 1)
                pe.wait_ge(ov_w, o * 48 + 48)
                wg, wu, wd = expert(0)
                for m, w in enumerate((wg, wu)):
                    for i in range(KF):
                        c = (m * KF + i) * CAP
                        wv = w.rearrange("p k (q i) -> p k i q", i=KF)
                        for k in range(KD):
                            mm = pe.matmul(ps[4][:, c:c + CAP], wv[:, k, i, :], XT[0][:, k, :], start=(k == 0),
                                           stop=(k == KD - 1))
                mm.then_inc(ov_gu, 1)
                pe.wait_ge(ov_hid, o + 1)
                for n in range(2):
                    for i in range(KF):
                        mm = pe.matmul(ps[n][0:CAP, :], HID[0][:, i, :], wd[:, i, n * 512:(n + 1) * 512],
                                       start=(i == 0), stop=(i == KF - 1))
                mm.then_inc(ov_y, 1)
            pe.wait_ge(y_evA, NE)
            pe.wait_ge(y_evV, NE)
            each_overflow(pe, overflow)

        @block.scalar
        def _(act):
            a = nc.scalar
            act.dma_start(cc, t["c"].rearrange("a (p k) -> (a p) k", k=KD)).then_inc(c_in, 16)
            act.dma_start(posi[:, :], t["positions"].rearrange("a (b p) -> (a p) b", p=P),
                          allow_slow_non_contiguous=True).then_inc(c_in, 16)
            act.dma_start(cg, pcol("g_pre_mix")).then_inc(pre_in, 16)
            act.dma_start(cb.rearrange("p (m k) -> p m k", m=2),
                          b_ada[0:2, :].rearrange("m (p k) -> p m k", k=KD)).then_inc(pre_in, 16)
            act.wait_ge(c_in, 32)
            a.activation(ctmp[:, 0:8], cc, ACT.Exp, scale=-1.0).then_inc(c_exp, 1)
            act.wait_ge(ang_ready, 1)
            a.activation(sinT[:, :], sinT[:, :], ACT.Sin).then_inc(trig_ready, 1)
            a.activation(cosT[:, :], cosT[:, :], ACT.Sin).then_inc(trig_ready, 1)
            act.wait_ge(x_in, 16)
            for b in range(NB):
                a.activation(xn[:, b, :], x3[:, b, :], ACT.Square, accum_out=ss1[:, b:b + 1]).then_inc(x_ss, 1)
            act.wait_ge(x_ss, NB)
            a.activation(r1, ss1, ACT.Sqrt, bias=eps, scale=1.0 / D).then_inc(x_sq, 1)
            act.wait_ge(x_r, 1)
            for b in range(NB):
                a.activation(xn[:, b, :], x3[:, b, :], ACT.Identity, bias=zero, scale=ss1[:, b:b + 1]).then_inc(x_n, 1)

            def bring(use, dst):
                act.wait_ge(tp_done, plan.tp[use] + 1)
                n = dst.shape[1] if len(dst.shape) == 2 else dst.shape[1] * dst.shape[2]
                src = bank(use)[:, 0:n]
                if len(dst.shape) == 3:
                    src = src.rearrange("p (c t) -> p c t", c=dst.shape[1])
                a.activation(dst, src, ACT.Copy).then_inc(evac, 1)

            act.wait_ge(gs_ready, 2)
            for k in range(KD):
                act.wait_ge(tp_done, k + 1)
                a.activation(hT3[:, k, :], bank(("x", k))[:, :], ACT.Identity, bias=sh1[:, k:k + 1],
                             scale=gs1[:, k:k + 1]).then_inc(evac, 1)
            act.dma_start(G1[:, :], prow(t["g_post_mix"], D)).then_inc(post_in, 16)
            act.dma_start(S2[:, :], prow(t["g_pre_ffn"], D)).then_inc(post_in, 16)
            act.dma_start(rb[:, 0:NG], prow(t["b_group"], NG)).then_inc(post_in, 16)
            act.dma_start(rb[:, NG:NG + NE], prow(t["b_expert"], NE)).then_inc(post_in, 16)

            into = {"qi": qiT, "qr": qrT, "kr": krT, "ka": kaT, "qa": qaT}
            for s in steps:
                if s in plan.v:
                    name, b = s[1:]
                    act.wait_ge(unit_done, plan.unit[s] + 1)
                    a.activation((vr if name == "vr" else va)[:, b, :], bank(s)[:, :], ACT.Copy).then_inc(v_ready, 1)
                elif s[0] == "unit" and s[1] == "gr":
                    act.wait_ge(unit_done, plan.unit[s] + 1)
                    a.activation(gr[:, s[2], :], bank(s)[:, :], ACT.Exp, scale=-1.0).then_inc(g_exp, 1)
                elif s[0] == "turn":
                    name, b = s[1:]
                    if name == "kw":
                        bring(s, kiT[:, b * P:(b + 1) * P])
                    else:
                        if (name, b) == ("qa", 0):
                            act.wait_ge(it_ready, NB * RHEADS)
                        bring(s, into[name][:, :, b * P:(b + 1) * P])
                elif s[0] == "IDX":
                    for u in range((NB - 1) * HEADS):
                        b, h = u // HEADS + 1, u % HEADS
                        n = (b + 1) * P
                        act.wait_ge(sc_done, u + 1)
                        if u >= 2:
                            act.wait_ge(relu_used, u - 1)
                        a.activation(RELU[u % 2][:, 0:n], bank(("idx", b, h))[:, 0:n], ACT.Relu).then_inc(relu_ready, 1)
                elif s[0] == "RET":
                    act.wait_ge(sc_done, (NB - 1) * HEADS)
                    for h in range(RHEADS):
                        act.wait_ge(o_done, h + 1)
                        a.activation(Rsb[:, :, h * RDH:(h + 1) * RDH],
                                     bank(("reto", h))[:, :].rearrange("p (b e) -> p b e", b=NB),
                                     ACT.Copy).then_inc(R_ready, 1)
                    act.wait_ge(ret_ss, 1)
                    a.activation(rr, ssr, ACT.Sqrt, bias=eps, scale=1.0 / RDH).then_inc(ret_sq, 1)
                elif s[0] == "RETT":
                    act.wait_ge(unit_done, len(plan.unit))
                    for b in range(NB):
                        bring(("rett", b), hT3[:, 4:8, b * P:(b + 1) * P])
                elif s[0] == "ATT":
                    for u in range(len(AHEADS) + 4):
                        if u < len(AHEADS):
                            b, h = AHEADS[u]
                            n = (b + 1) * P
                            act.wait_ge(att_max, u + 1)
                            if u >= 2:
                                act.wait_ge(tp_done, plan.tp[("pt",) + AHEADS[u - 2]] + 1)
                            a.activation(PEX[u % 2][:, 0:n], SMX[u % 2][:, 0:n], ACT.Exp, bias=nmx[:, u % 2:u % 2 + 1],
                                         scale=-1.0, accum_out=rsum[:, b, h:h + 1]).then_inc(att_exp, 1)
                        if 2 <= u < len(AHEADS) + 2:
                            b, h = AHEADS[u - 2]
                            if u >= 4:
                                act.wait_ge(o_done, RHEADS + u - 3)
                            bring(("pt", b, h), PTS[u % 2][:, 0:(b + 1) * P])
                        if u >= 4 and AHEADS[u - 4][1] == HEADS - 1:
                            b = AHEADS[u - 4][0]
                            bring(("attt", b), hT3[:, 0:4, b * P:(b + 1) * P])
                    act.dma_start(G2, prow(t["g_post_ffn"], D)).then_inc(g2_in, 16)
                elif s[0] == "OUT":
                    for b in range(NB + 1):
                        if b < NB:
                            w = plan.bank[("wout", b)] * 512
                            act.wait_ge(wout_done, b + 1)
                            a.activation(JUNK, psum[:, w:w + D], ACT.Square, accum_out=ssm[:, b:b + 1]).then_inc(mix_ss, 1)
                            act.wait_ge(mix_ss, b + 1)
                            a.activation(rm[:, b:b + 1], ssm[:, b:b + 1], ACT.Sqrt, bias=eps,
                                         scale=1.0 / D).then_inc(mix_sq, 1)
                        if b >= 1:
                            if b >= 3:
                                act.wait_ge(router_done, b - 2)
                            for q in range(2):
                                bring(("h2", b - 1, q), H2T[(b - 1) % 2][:, 4 * q:4 * q + 4, :])
                        if b < NB:
                            act.wait_ge(res_ready, b + 1)
                            a.activation(JUNK, x3[:, b, :], ACT.Square, accum_out=ss2[:, b:b + 1]).then_inc(res_ss, 1)
                            act.wait_ge(res_ss, b + 1)
                            a.activation(r2[:, b:b + 1], ss2[:, b:b + 1], ACT.Sqrt, bias=eps,
                                         scale=1.0 / D).then_inc(res_sq, 1)
                    act.wait_ge(g_sub, 1)
                    a.activation(GEXV, GSUBV, ACT.Exp).then_inc(g_exped, 1)
                    act.wait_ge(d_sub, 1)
                    a.activation(P2, DSUB, ACT.Exp).then_inc(d_exped, 1)

            def turned(e, par):
                if not (isinstance(e, int) and e < 2):
                    act.wait_ge(gu_mm, e - 1)
                for q in range(2):
                    act.wait_ge(xt_mm, 2 * e + 1 + q)
                    a.activation(XT[par][:, 4 * q:4 * q + 4, :],
                                 ps[2 + q][:, 0:4 * CAP].rearrange("p (k c) -> p k c", k=4), ACT.Copy).then_inc(xt_ev, 1)

            def gated(e, par):
                act.wait_ge(gu_mm, e + 1)
                if not (isinstance(e, int) and e < 2):
                    act.wait_ge(hid_ready, e - 1)
                a.activation(EG[par], ps[4 + par][:, 0:W2], ACT.Exp, scale=-1.0).then_inc(gu_exp, 1)

            def downed(e, par):
                act.wait_ge(y_mm, 2 * e + 1)
                if not (isinstance(e, int) and e < 2):
                    act.wait_ge(y_out[par], 8 * (e - par))
                a.activation(YO[par][:, 0:512], ps[(0, 6)[par]][0:CAP, :], ACT.Copy).then_inc(y_evA, 1)

            turned(0, 0)
            turned(1, 1)
            gated(0, 0)

            def experts(base, last):
                for j in range(RING):
                    e = base + j
                    if not (last and j == RING - 1):
                        gated(e + 1, (j + 1) % 2)
                    if not (last and j >= RING - 2):
                        turned(e + 2, j % 2)
                    downed(e, j % 2)

            experts(0, False)
            with act.Fori(1, NE // RING - 1) as i:
                experts(i * RING, False)
            experts(NE - RING, True)

            def overflow(o):
                act.wait_ge(ov_turned, o + 1)
                for q in range(2):
                    ins = a.activation(XT[0][:, 4 * q:4 * q + 4, :],
                                       ps[2 + q][:, 0:4 * CAP].rearrange("p (k c) -> p k c", k=4), ACT.Copy)
                ins.then_inc(ov_brought, 1)
                act.wait_ge(ov_gu, o + 1)
                a.activation(EG[0], ps[4][:, 0:W2], ACT.Exp, scale=-1.0).then_inc(ov_exp, 1)
                act.wait_ge(ov_y, o + 1)
                a.activation(YO[0][:, 0:512], ps[0][0:CAP, :], ACT.Copy).then_inc(ov_evA, 1)
            act.wait_ge(y_out[0], 8 * NE)
            each_overflow(act, overflow)

            act.wait_ge(y_base, 1)
            rows = y_dram.rearrange("(b p j) d -> b p j d", b=NB, j=2)
            for b in range(NB):
                act.dma_start(YG[b], rows[b]).then_inc(y_back[b], 16)
            for b in range(NB):
                act.wait_ge(yw_ready, b + 1)
                a.activation(JUNK2, YG[b][:, 0, :], ACT.Square, accum_out=yss[:, b:b + 1]).then_inc(y_ss, 1)
                act.wait_ge(y_ss, b + 1)
                a.activation(yr[:, b:b + 1], yss[:, b:b + 1], ACT.Sqrt, bias=eps, scale=1.0 / D).then_inc(y_sq, 1)

        @block.vector
        def _(dve):
            v = nc.vector
            chained = [0]

            def link(ins):
                chained[0] += 1
                ins.then_inc(v_chain, 1)
                dve.wait_ge(v_chain, chained[0])

            def relay(ins, s, n):
                ins.then_inc(s, 1)
                dve.wait_ge(s, n)

            dve.wait_ge(cst_in, 16)
            dve.wait_ge(c_in, 32)
            link(v.tensor_copy(posf, posi[:, :]))
            for b in range(NB):
                last = v.tensor_scalar(sinT[:, b * 64:(b + 1) * 64], cst[:, C_FREQ:C_FREQ + 64], posf[:, b:b + 1], None,
                                       ALU.mult)
            link(last)
            link(v.tensor_scalar(cosT[:, :], sinT[:, :], 1.0 / (2 * math.pi), MAGIC, ALU.mult, ALU.add))
            link(v.tensor_scalar(cosT[:, :], cosT[:, :], MAGIC, None, ALU.subtract))
            for part in TWO_PI:
                link(v.scalar_tensor_tensor(out=sinT[:, :], in0=cosT[:, :], scalar=-part, in1=sinT[:, :], op0=ALU.mult,
                                            op1=ALU.add))
            link(v.tensor_scalar(sinT[:, :], sinT[:, :], 3.1415925, -3.1415925, ALU.min, ALU.max))
            link(v.scalar_tensor_tensor(out=cosT[:, :], in0=sinT[:, :], scalar=-1.0, in1=sinT[:, :], op0=ALU.mult,
                                        op1=ALU.min))
            v.tensor_scalar(cosT[:, :], cosT[:, :], math.pi / 2, None, ALU.add).then_inc(ang_ready, 1)
            dve.wait_ge(c_exp, 1)
            link(v.tensor_scalar(ctmp[:, 8:16], ctmp[:, 0:8], 1.0, None, ALU.add))
            link(v.reciprocal(ctmp[:, 0:8], ctmp[:, 8:16]))
            link(v.tensor_tensor(sc_, cc, ctmp[:, 0:8], ALU.mult))

            def ada(i, piece, pieces):
                m, half = i // 2, i % 2
                acc = (accA[:, m, :] if m < 2 else accB[:, :])[:, half * 512:(half + 1) * 512]
                w = chunk(AT[("ada", i)])
                if piece == 0:
                    land(dve, AT[("ada", i)])
                    if m >= 2 and half == 0:
                        dve.wait_ge(bias_in, 16 * (m - 1))
                for k in range(piece * KD // pieces, (piece + 1) * KD // pieces):
                    if m < 2 and k == 0:
                        ins = v.tensor_scalar(acc, w[:, 0, :], sc_[:, 0:1], None, ALU.mult)
                    else:
                        ins = v.scalar_tensor_tensor(out=acc, in0=w[:, k, :], scalar=sc_[:, k:k + 1], in1=acc,
                                                     op0=ALU.mult, op1=ALU.add)
                    if k < KD - 1:
                        link(ins)
                if piece == pieces - 1:
                    ins.then_inc(ada_done, 1)

            v.memset(accB[:, :], 0.0).then_inc(accB_clear, 1)
            for i in range(4):
                if i == 2:
                    dve.wait_ge(x_sq, 1)
                    v.reciprocal(ss1, r1).then_inc(x_r, 1)
                ada(i, 0, 1)
            dve.wait_ge(pre_in, 32)
            dve.wait_ge(modA_done, 2)
            o = bank(("modA",))
            v.tensor_tensor(sh1, o[:, 0:KD], cb[:, 0:KD], ALU.add).then_inc(gs_ready, 1)
            link(v.tensor_tensor(modA_s[:, 0:KD], o[:, KD:2 * KD], cb[:, KD:2 * KD], ALU.add))
            v.scalar_tensor_tensor(out=gs1, in0=modA_s[:, 0:KD], scalar=1.0, in1=cg, op0=ALU.add,
                                   op1=ALU.mult).then_inc(gs_ready, 1)

            def rotate(s):
                name, b = s[1:]
                r, d = plan.rope[s], ROPE[name]
                width = 64 if name == "kw" else 512
                heads, hd = width // d, d // 2
                dve.wait_ge(unit_done, plan.unit[s] + 1)
                if r == 0:
                    dve.wait_ge(trig_ready, 2)
                else:
                    dve.wait_ge(roped, r)
                src = bank(s)[:, 0:width].rearrange("p (h a i) -> p h a i", h=heads, a=2)
                for n, tab in enumerate((cosT, sinT)):
                    tb = tab[:, b * 64:(b + 1) * 64].rearrange("p (i e) -> p i e", e=64 // hd)[:, :, 0]
                    tb = tb.unsqueeze(1).unsqueeze(1).to_broadcast([P, heads, 2, hd])
                    dst = ropebuf[:, n * 512:n * 512 + width].rearrange("p (h a i) -> p h a i", h=heads, a=2)
                    if n == 1 and name == "kw":
                        v.tensor_scalar(wi[:, b, :], bank(s)[:, DH:KW], IDX_SCALE, None, ALU.mult)
                    ins = v.tensor_tensor(dst, src, tb, ALU.mult)
                ins.then_inc(rope_ab, 1)

            def mask_of(b):
                at = (None, 0, 256, 640)[b]
                return cst[:, C_CAUSAL:C_CAUSAL + P] if b == 0 else score[:, at:at + (b + 1) * P]

            def topk():
                for b in range(1, NB):
                    m = mask_of(b)
                    for r in range(TOPK // 8):
                        link(v.max(top8, m))
                        link(v.match_replace(m, top8, m, TAKEN))
                        if r == TOPK // 8 - 1:
                            link(v.tensor_scalar(m, m, TAKEN / 2, NEG, ALU.is_gt, ALU.mult))
                        yield

            rounds = topk()

            def select_keys(n):
                for _ in range(n):
                    next(rounds, None)

            def first_best(x, best, marks, least, numbers, n, chosen):
                link(v.tensor_reduce(best.rearrange("p b n -> p (b n)"), x, AX, ALU.max))
                link(v.tensor_tensor(marks, x, best.to_broadcast([P, NB, n]), ALU.is_equal))
                link(v.scalar_tensor_tensor(out=marks, in0=numbers, scalar=float(-n), in1=marks, op0=ALU.add,
                                            op1=ALU.mult))
                link(v.tensor_reduce(least.rearrange("p b n -> p (b n)"), marks, AX, ALU.min))
                link(v.tensor_tensor(chosen, marks, least.to_broadcast([P, NB, n]), ALU.is_equal))

            def routing():
                def numbers(n):
                    return cst[:, C_IOTA:C_IOTA + n].unsqueeze(1).to_broadcast([P, NB, n])

                def flat(x):
                    return x.rearrange("p b n -> p (b n)")

                dve.wait_ge(router_done, NB)
                relay(v.tensor_tensor(LG, bank(("router",))[:, 0:144].rearrange("p (b n) -> p b n", b=NB),
                                      rb[:, :].unsqueeze(1).to_broadcast([P, NB, NG + NE]), ALU.add), lg_ready, 1)
                first_best(LG[:, :, 0:NG], GMAX, GT, GM, numbers(NG), NG, SG)
                v.tensor_tensor(GSUBV, LG[:, :, 0:NG], GMAX.to_broadcast([P, NB, NG]), ALU.subtract).then_inc(g_sub, 1)
                prod = retbuf[:, 384:512].rearrange("p (b e g) -> p b e g", b=NB, e=EPG)
                for b in range(NB):
                    last = v.tensor_tensor(prod[:, b, :, :], LG[:, b, NG:].rearrange("p (g e) -> p e g", g=NG),
                                           SG[:, b, :].unsqueeze(1).to_broadcast([P, EPG, NG]), ALU.mult)
                link(last)
                link(v.tensor_reduce(flat(EL), retbuf[:, 384:512].rearrange("p (q g) -> p q g", g=NG), AX, ALU.add))
                first_best(EL, EMAX, ET, EM, numbers(EPG), EPG, O1)
                link(v.scalar_tensor_tensor(out=EL2, in0=O1, scalar=NEG, in1=EL, op0=ALU.mult, op1=ALU.add))
                first_best(EL2, EMAX2, ET, EM, numbers(EPG), EPG, O2)
                v.tensor_tensor(flat(DSUB), flat(EMAX2), flat(EMAX), ALU.subtract).then_inc(d_sub, 1)
                for b in range(NB):
                    for oh, o in ((OH1, O1), (OH2, O2)):
                        last = v.tensor_tensor(oh[:, b, :].rearrange("p (g e) -> p g e", g=NG),
                                               SG[:, b, :].unsqueeze(2).to_broadcast([P, NG, EPG]),
                                               o[:, b, :].unsqueeze(1).to_broadcast([P, NG, EPG]), ALU.mult)
                link(last)
                v.tensor_tensor(OH, OH1, OH2, ALU.add).then_inc(oh_ready, 1)
                dve.wait_ge(g_exped, 1)
                link(v.tensor_reduce(flat(GSUM), GEXV, AX, ALU.add))
                link(v.reciprocal(flat(GTOP), flat(GSUM)))
                dve.wait_ge(d_exped, 1)
                link(v.tensor_scalar(flat(WT), flat(P2), 1.0, None, ALU.add))
                link(v.reciprocal(flat(DSUB), flat(WT)))
                link(v.tensor_tensor(wts[:, :, 0:1], DSUB, GTOP, ALU.mult))
                v.tensor_tensor(wts[:, :, 1:2], wts[:, :, 0:1], P2, ALU.mult)
                dve.wait_ge(rank_done, 1)
                o = bank(("rank",))
                v.tensor_copy(flat(RANK), o[:, 0:NB * NE])
                link(v.tensor_copy(CNT, o[:, NB * NE:(NB + 1) * NE]))
                link(v.tensor_scalar(MFL, RANK, float(CAP), None, ALU.is_ge))
                link(v.tensor_scalar(OV, CNT, float(CAP), None, ALU.is_gt))
                for m in range(2, NM):
                    v.scalar_tensor_tensor(out=MFL, in0=RANK, scalar=float(m * CAP), in1=MFL, op0=ALU.is_ge,
                                           op1=ALU.add).then_inc(v_chain, 1)
                    v.scalar_tensor_tensor(out=OV, in0=CNT, scalar=float(m * CAP), in1=OV, op0=ALU.is_gt,
                                           op1=ALU.add).then_inc(v_chain, 1)
                    chained[0] += 2
                    dve.wait_ge(v_chain, chained[0])
                link(v.tensor_tensor_scan(BINC, ones[:, 0:NE], OV, 0.0, ALU.mult, ALU.add))
                v.tensor_tensor(OVC, BINC.unsqueeze(1).to_broadcast([P, NOV, NE]),
                                cst[:, C_IOTA:C_IOTA + NOV].unsqueeze(2).to_broadcast([P, NOV, NE]), ALU.is_le)
                link(v.tensor_tensor(BEX, BINC, OV, ALU.subtract))
                link(v.tensor_tensor(BEX, BEX, cst[:, C_IOTA:C_IOTA + NE], ALU.subtract))
                link(v.tensor_reduce(EO, OVC, AX, ALU.add))
                link(v.tensor_scalar(EO, EO, float(NE - 1), None, ALU.min))
                v.tensor_copy(ctl[:, 0:NOV], EO)
                v.tensor_copy(ctl[:, NOV:NOV + 1], BINC[:, NE - 1:NE]).then_inc(ctl_ready, 1)
                link(v.scalar_tensor_tensor(out=QT, in0=MFL, scalar=float(NE - 1),
                                            in1=BEX.unsqueeze(1).to_broadcast([P, NB, NE]), op0=ALU.add, op1=ALU.add))
                link(v.scalar_tensor_tensor(out=QT, in0=MFL, scalar=0.0, in1=QT, op0=ALU.is_gt, op1=ALU.mult))
                link(v.tensor_tensor(QT, QT, numbers(NE), ALU.add))
                link(v.scalar_tensor_tensor(out=MFL, in0=MFL, scalar=float(-CAP), in1=RANK, op0=ALU.mult,
                                            op1=ALU.add))
                for j, oh in enumerate((OH1, OH2)):
                    for of, place in ((QT, TILE), (MFL, ROW)):
                        link(v.tensor_tensor(TMP, oh, of, ALU.mult))
                        link(v.tensor_reduce(place[:, :, j], TMP, AX, ALU.add))
                def in_pairs(x, n):
                    return x.rearrange("p b j -> p (b j)").unsqueeze(2).to_broadcast([P, 2 * NB, n])

                def iota(n):
                    return cst[:, C_IOTA:C_IOTA + n].unsqueeze(1).to_broadcast([P, 2 * NB, n])

                link(v.tensor_tensor(IN_TILE, in_pairs(TILE, NT), iota(NT), ALU.is_equal))
                v.tensor_tensor(IN_ROW, in_pairs(ROW, CAP), iota(CAP), ALU.is_equal)
                v.tensor_tensor(IN_TILE, IN_TILE, cst[:, C_PAIR:C_PAIR + 2 * NB].unsqueeze(2).to_broadcast(
                    [P, 2 * NB, NT]), ALU.mult).then_inc(slot_ready, 1)
                dve.wait_ge(table_done, 1)
                o = bank(("table",))[0:CAP, 0:NT]
                link(v.tensor_scalar(EMPTY, o, 0.0, float(NOBODY), ALU.is_equal, ALU.mult))
                link(v.scalar_tensor_tensor(out=IDS, in0=o, scalar=-1.0, in1=EMPTY, op0=ALU.add, op1=ALU.add))
                link(v.tensor_copy(pid_t[0:CAP, :], IDS))
                v.tensor_scalar(tok_t[0:CAP, :], pid_t[0:CAP, :], 1, None, ALU.logical_shift_right).then_inc(tok_ready, 1)

            for s in steps:
                if s in plan.rope:
                    rotate(s)
                    if s[1] in ("kr", "ka", "qa"):
                        select_keys(2)
                elif s in plan.v:
                    select_keys(2)
                elif s[0] == "unit":
                    b = s[2]
                    dve.wait_ge(g_exp, b + 1)
                    link(v.tensor_scalar(gr[:, b, :], gr[:, b, :], 1.0, None, ALU.add))
                    link(v.reciprocal(gr[:, b, :], gr[:, b, :]))
                    v.tensor_tensor(gr[:, b, :], bank(s)[:, :], gr[:, b, :], ALU.mult).then_inc(g_ready, 1)
                    select_keys(2)
                elif s[0] == "IDX":
                    for u in range((NB - 1) * HEADS):
                        b, h = u // HEADS + 1, u % HEADS
                        m, n = mask_of(b), (b + 1) * P
                        dve.wait_ge(relu_ready, u + 1)
                        r = RELU[u % 2][:, 0:n]
                        if h == 0:
                            relay(v.tensor_scalar(m, r, wi[:, b, h:h + 1], None, ALU.mult), relu_used, u + 1)
                        else:
                            relay(v.scalar_tensor_tensor(out=m, in0=r, scalar=wi[:, b, h:h + 1], in1=m, op0=ALU.mult,
                                                         op1=ALU.add), relu_used, u + 1)
                        if h == HEADS - 1:
                            link(v.tensor_tensor(m[:, b * P:n], m[:, b * P:n], cst[:, C_CAUSAL:C_CAUSAL + P], ALU.add))
                elif s[0] == "RET":
                    dve.wait_ge(decay_in, 16)
                    for h in range(RHEADS):
                        if h >= 2:
                            dve.wait_ge(o_done, h - 1)
                        for j in range(NB):
                            n = S - j * P
                            dve.wait_ge(sc_done, plan.sc[("ret", h, j)] + 1)
                            v.tensor_tensor(iT(h, j), bank(("ret", h, j))[:, 0:n], decay[:, h, 0:n],
                                            ALU.mult).then_inc(it_ready, 1)
                    dve.wait_ge(R_ready, RHEADS)
                    sq = retbuf[:, 0:2048]
                    flat = work[:, 6144:8192]
                    link(v.tensor_tensor(sq, flat, flat, ALU.mult))
                    v.tensor_reduce(ssr, sq.rearrange("p (g e) -> p g e", g=16), AX, ALU.add).then_inc(ret_ss, 1)
                    dve.wait_ge(ret_sq, 1)
                    link(v.reciprocal(ssr, rr))
                    for b in range(NB):
                        for h in range(RHEADS):
                            e = slice(h * RDH, (h + 1) * RDH)
                            ins = v.scalar_tensor_tensor(out=Rsb[:, b, e], in0=Rsb[:, b, e],
                                                         scalar=ssr[:, b * 4 + h:b * 4 + h + 1], in1=gr[:, b, e],
                                                         op0=ALU.mult, op1=ALU.mult)
                        ins.then_inc(ret_ready, 1)
                elif s[0] == "MOD":
                    m = s[1]
                    dve.wait_ge(mod_done, 2 * (m - 2) + 2)
                    if m < 5:
                        v.memset(accB[:, :], 0.0).then_inc(accB_clear, 1)
                    if m == 2:
                        dve.wait_ge(post_in, 64)
                    for n in range(2):
                        c = slice(n * 512, (n + 1) * 512)
                        o = bank(("MOD", m, n))
                        if m == 2:
                            ins = v.tensor_tensor(G1[:, c], o, G1[:, c], ALU.mult)
                        elif m == 3:
                            ins = v.tensor_copy(T2[:, c], o)
                        elif m == 4:
                            ins = v.scalar_tensor_tensor(out=S2[:, c], in0=o, scalar=1.0, in1=S2[:, c], op0=ALU.add,
                                                         op1=ALU.mult)
                        else:
                            dve.wait_ge(g2_in, 16)
                            ins = v.tensor_tensor(G2[:, c], o, G2[:, c], ALU.mult)
                        ins.then_inc(mod_ready, 1)
                elif s[0] == "ATT":
                    select_keys(1000)
                    for u in range(len(AHEADS) + 4):
                        if u < len(AHEADS):
                            b, h = AHEADS[u]
                            n = (b + 1) * P
                            dve.wait_ge(sc_done, plan.sc[("att", b, h)] + 1)
                            if u >= 2:
                                dve.wait_ge(att_exp, u - 1)
                            v.tensor_tensor_reduce(SMX[u % 2][:, 0:n], bank(("att", b, h))[:, 0:n], mask_of(b),
                                                   -ATT_SCALE, 3.0e38, ALU.add, ALU.min,
                                                   nmx[:, u % 2:u % 2 + 1]).then_inc(att_max, 1)
                        if u >= 4 and AHEADS[u - 4][1] == HEADS - 1:
                            b = AHEADS[u - 4][0]
                            dve.wait_ge(att_exp, u - 3)
                            link(v.reciprocal(rinv, rsum[:, b, :]))
                            dve.wait_ge(o_done, RHEADS + u - 3)
                            if b >= 2:
                                dve.wait_ge(tp_done, plan.tp[("attt", b - 2)] + 1)
                            v.tensor_tensor(ATO[b % 2].rearrange("p (h e) -> p h e", h=HEADS),
                                            bank(("atto", b))[:, :].rearrange("p (h e) -> p h e", h=HEADS),
                                            rinv.unsqueeze(2).to_broadcast([P, HEADS, DH]),
                                            ALU.mult).then_inc(att_ready, 1)
                elif s[0] == "OUT":
                    for b in range(NB):
                        w = plan.bank[("wout", b)] * 512
                        dve.wait_ge(mix_sq, b + 1)
                        link(v.reciprocal(ssm[:, b:b + 1], rm[:, b:b + 1]))
                        if b == 0:
                            dve.wait_ge(mod_ready, 8)
                        relay(v.scalar_tensor_tensor(out=MIXN[b % 2], in0=psum[:, w:w + D], scalar=ssm[:, b:b + 1],
                                                     in1=G1[:, :], op0=ALU.mult, op1=ALU.mult), mix_n, b + 1)
                        v.tensor_tensor(x3[:, b, :], x3[:, b, :], MIXN[b % 2], ALU.add).then_inc(res_ready, 1)
                        dve.wait_ge(res_sq, b + 1)
                        link(v.reciprocal(ss2[:, b:b + 1], r2[:, b:b + 1]))
                        if b >= 2:
                            dve.wait_ge(tp_done, plan.tp[("h2", b - 2, 1)] + 1)
                            dve.wait_ge(h2_out[b % 2], 16)
                        link(v.scalar_tensor_tensor(out=H2[b % 2], in0=x3[:, b, :], scalar=ss2[:, b:b + 1],
                                                    in1=S2[:, :], op0=ALU.mult, op1=ALU.mult))
                        v.tensor_tensor(H2[b % 2], H2[b % 2], T2[:, :], ALU.add).then_inc(h2_ready, 1)
                    routing()
                if s[0] == "unit":
                    kind, i = ITEMS[AT[("in", s[1])] + 1]
                    if kind == "ada":
                        ada(i, s[2], NB)

            def gate(e, par):
                dve.wait_ge(gu_exp, e + 1)
                g = ps[4 + par]
                v.tensor_scalar(EG[par], EG[par], 1.0, None, ALU.add).then_inc(gu_step, 1)
                dve.wait_ge(gu_step, 3 * e + 1)
                v.reciprocal(EG[par], EG[par]).then_inc(gu_step, 1)
                dve.wait_ge(gu_step, 3 * e + 2)
                v.tensor_tensor(EG[par], g[:, 0:W2], EG[par], ALU.mult).then_inc(gu_step, 1)
                dve.wait_ge(gu_step, 3 * e + 3)
                v.tensor_tensor(HID[par].rearrange("p i c -> p (i c)"), g[:, W2:2 * W2], EG[par],
                                ALU.mult).then_inc(hid_ready, 1)

            def downed(e, par):
                dve.wait_ge(y_mm, 2 * e + 2)
                if not (isinstance(e, int) and e < 2):
                    dve.wait_ge(y_out[par], 8 * (e - par))
                v.tensor_copy(YO[par][:, 512:1024], ps[(0, 6)[par] + 1][0:CAP, :]).then_inc(y_evV, 1)

            gate(0, 0)

            def experts(base, last):
                for j in range(RING):
                    if not (last and j == RING - 1):
                        gate(base + (j + 1), (j + 1) % 2)
                    downed(base + j, j % 2)

            experts(0, False)
            with dve.Fori(1, NE // RING - 1) as i:
                experts(i * RING, False)
            experts(NE - RING, True)

            def overflow(o):
                dve.wait_ge(ov_exp, o + 1)
                v.tensor_scalar(EG[0], EG[0], 1.0, None, ALU.add).then_inc(ov_step, 1)
                dve.wait_ge(ov_step, o * 3 + 1)
                v.reciprocal(EG[0], EG[0]).then_inc(ov_step, 1)
                dve.wait_ge(ov_step, o * 3 + 2)
                v.tensor_tensor(EG[0], ps[4][:, 0:W2], EG[0], ALU.mult).then_inc(ov_step, 1)
                dve.wait_ge(ov_step, o * 3 + 3)
                v.tensor_tensor(HID[0].rearrange("p i c -> p (i c)"), ps[4][:, W2:2 * W2], EG[0],
                                ALU.mult).then_inc(ov_hid, 1)
                dve.wait_ge(ov_y, o + 1)
                v.tensor_copy(YO[0][:, 512:1024], ps[1][0:CAP, :]).then_inc(ov_evV, 1)
            dve.wait_ge(y_out[0], 8 * NE)
            each_overflow(dve, overflow)

            for b in range(NB + 1):
                if b < NB:
                    y = YG[b]
                    dve.wait_ge(y_back[b], 16)
                    link(v.tensor_scalar(y[:, 1, :], y[:, 1, :], wts[:, b, 1:2], None, ALU.mult))
                    relay(v.scalar_tensor_tensor(out=y[:, 0, :], in0=y[:, 0, :], scalar=wts[:, b, 0:1], in1=y[:, 1, :],
                                                 op0=ALU.mult, op1=ALU.add), yw_ready, b + 1)
                if b >= 1:
                    q, y = b - 1, YG[b - 1]
                    dve.wait_ge(y_sq, q + 1)
                    link(v.reciprocal(yss[:, q:q + 1], yr[:, q:q + 1]))
                    link(v.scalar_tensor_tensor(out=y[:, 1, :], in0=y[:, 0, :], scalar=yss[:, q:q + 1], in1=G2,
                                                op0=ALU.mult, op1=ALU.mult))
                    v.tensor_tensor(y[:, 1, :], y[:, 1, :], x3[:, q, :], ALU.add).then_inc(o_add, 1)

        @block.gpsimd
        def _(pool):
            g = nc.gpsimd

            def rotate(s):
                name, b = s[1:]
                r, d = plan.rope[s], ROPE[name]
                width = 64 if name == "kw" else 512
                heads = width // d
                at = 1024 + (r % 2) * 512
                pool.wait_ge(rope_ab, r + 1)
                if r >= 2:
                    pool.wait_ge(tp_done, plan.tp[turns[r - 2]] + 1)
                xc, xs_ = (ropebuf[:, n * 512:n * 512 + width].rearrange("p (h a i) -> p h a i", h=heads, a=2)
                           for n in range(2))
                for copy in range(2 if name == "kw" else 1):
                    dst = ropebuf[:, at + copy * 64:at + copy * 64 + width].rearrange("p (h a i) -> p h a i", h=heads,
                                                                                      a=2)
                    g.tensor_tensor(dst[:, :, 0, :], xc[:, :, 0, :], xs_[:, :, 1, :], ALU.subtract)
                    ins = g.tensor_tensor(dst[:, :, 1, :], xc[:, :, 1, :], xs_[:, :, 0, :], ALU.add)
                ins.then_inc(roped, 1)

            def bias(m):
                pool.wait_ge(accB_clear, m - 1)
                pool.dma_start(accB[0:1, :], b_ada[m:m + 1, :]).then_inc(bias_in, 16)

            turns = [("turn",) + s[1:] for s in plan.rope]
            bias(2)
            for s in steps:
                if s in plan.rope:
                    rotate(s)
                if s[0] == "MOD" and s[1] < 5:
                    bias(s[1] + 1)
            for b in range(NB):
                pool.wait_ge(h2_ready, b + 1)
                pool.dma_start(h2_dram[b * P:(b + 1) * P, :], H2[b % 2]).then_inc(h2_out[b % 2], 16)
            pool.wait_ge(h2_out[0], 16 * (NB // 2))
            pool.wait_ge(h2_out[1], 16 * (NB // 2))
            pool.wait_ge(tok_ready, 1)

            token_bound, pair_bound = g.to_reg(S - 1), g.to_reg(2 * S - 1)

            def gather(e, s):
                first = isinstance(e, int) and e < RING
                if not first:
                    pool.wait_ge(xt_mm, 2 * e + (2 - 2 * RING))
                    pool.wait_ge(xg_in[s], 4 * (e - s))
                g.tensor_copy(gix[0:CAP, s:s + 1], col(tok_t, e)).then_inc(ix_ready, 1)
                pool.wait_ge(ix_ready, e + 1 if first else 2 * e + (1 - RING))
                pool.sem_inc(pool_steps, 1)
                g.indirect_dma_start(out=XG[s], out_offset=None, in_=h2_dram,
                                     in_offset=bass.IndirectOffsetOnAxis(ap=gix[0:CAP, s:s + 1], axis=0),
                                     bounds_check=token_bound, oob_is_err=False).then_inc(xg_in[s], 16)

            def scatter(e, par, ahead):
                pool.wait_ge(y_evA, e + 1)
                pool.wait_ge(y_evV, e + 1)
                if not (isinstance(e, int) and e < 2):
                    pool.wait_ge(y_out[par], 8 * (e - par))
                g.tensor_copy(six[0:CAP, par:par + 1], col(pid_t, e)).then_inc(ix_ready, 1)
                pool.wait_ge(ix_ready, e + 1 + ahead)
                pool.sem_inc(pool_steps, 1)
                g.indirect_dma_start(out=y_dram, out_offset=bass.IndirectOffsetOnAxis(ap=six[0:CAP, par:par + 1], axis=0),
                                     in_=YO[par], in_offset=None, bounds_check=pair_bound,
                                     oob_is_err=False).then_inc(y_out[par], 16)

            for s in range(RING):
                gather(s, s)

            def experts(base, last):
                for j in range(RING):
                    e = base + j
                    if not last:
                        gather(e + RING, j)
                        scatter(e, j % 2, e + RING + 1)
                    else:
                        scatter(e, j % 2, NE)

            experts(0, False)
            with pool.Fori(1, NE // RING - 1) as i:
                experts(i * RING, False)
            experts(NE - RING, True)
            pool.wait_ge(y_out[0], 8 * NE)
            pool.wait_ge(y_out[1], 8 * NE)
            pool.sem_inc(ov_go, 1)

            def overflow(o):
                pool.wait_ge(ov_go, o + 1)
                g.tensor_copy(gix[0:CAP, 0:1], col(tok_t, o + NE)).then_inc(ov_ix, 1)
                g.tensor_copy(six[0:CAP, 0:1], col(pid_t, o + NE)).then_inc(ov_ix, 1)
                pool.wait_ge(ov_ix, o * 2 + 2)
                pool.sem_inc(pool_steps, 1)
                g.indirect_dma_start(out=XG[0], out_offset=None, in_=h2_dram,
                                     in_offset=bass.IndirectOffsetOnAxis(ap=gix[0:CAP, 0:1], axis=0),
                                     bounds_check=token_bound, oob_is_err=False).then_inc(ov_x, 16)
                pool.wait_ge(ov_evA, o + 1)
                pool.wait_ge(ov_evV, o + 1)
                pool.sem_inc(pool_steps, 1)
                g.indirect_dma_start(out=y_dram, out_offset=bass.IndirectOffsetOnAxis(ap=six[0:CAP, 0:1], axis=0),
                                     in_=YO[0], in_offset=None, bounds_check=pair_bound,
                                     oob_is_err=False).then_inc(ov_out, 16)
                pool.wait_ge(ov_out, o * 16 + 16)
                pool.sem_inc(ov_go, 1)
            each_overflow(pool, overflow)
            pool.sem_inc(y_base, 1)


def col(tab, e):
    return tab[0:CAP, e:e + 1] if isinstance(e, int) else tab[0:CAP, bass.ds(e, 1)]


INPUTS = ["x", "c", "positions", "g_pre_mix", "w_ada", "b_ada", "w_in", "w_out", "g_post_mix", "g_pre_ffn", "w_group",
          "b_group", "w_expert", "b_expert", "w_gate_exp", "w_up_exp", "w_down_exp", "g_post_ffn"]


def kernel(**inputs):
    import concourse.bacc as bacc
    from concourse.bass_utils import run_bass_kernel_spmd

    nc = bacc.Bacc("TRN2", target_bir_lowering=False, num_devices=1)
    cst, decay = shape_constants()
    given = {name: np.ascontiguousarray(inputs[name]) for name in INPUTS}
    given.update(cst=cst, decay=decay)
    arrays, tensors = {}, {}
    for name, a in given.items():
        arrays[f"in_{name}"] = a
        tensors[name] = nc.dram_tensor(f"in_{name}", a.shape, mybir.dt.from_np(a.dtype), kind="ExternalInput").ap()
    out = nc.dram_tensor("out", (1, S, D), F32, kind="ExternalOutput").ap()
    build(nc, tensors, out)
    r = run_bass_kernel_spmd(nc, [arrays], core_ids=[0])
    return r.results[0]["out"]
```
